# Optimizing a Trainium2 kernel written in Bass

```python
import math
import jax, jax.numpy as jnp
from jax import lax
import numpy as np

D_MODEL = 1024
BATCH = 1
SEQ = 256
DEPTH = 2
DEC_BATCH = 8
DEC_SEQ = 4
PAST_LEN = 2048
PAGE_SIZE = 128

MIX_A = D_MODEL // 2
SSM_GROUP = 16
NG_A = MIX_A // SSM_GROUP
SSM_STATE = 64
MIX_B = D_MODEL - MIX_A
HD_B = 64
NH_B = MIX_B // HD_B
CHUNK = 128
MIX_WIDTH = MIX_A + MIX_B
IN_WIDTH = MIX_A + 2 * MIX_B
D_FF = ((8 * D_MODEL // 3 + 63) // 64) * 64
N_EXPERTS = 8
TOP_K = 2
D_FF_EXPERT = D_FF // 2
N_DENSE = (DEPTH + 1) // 2
N_MOE = DEPTH // 2
EPS = 1e-6
DT_MIN = 1e-3
DT_MAX = 1e-1

kernel_name = "hybrid_s5_gmlp_decoder_step"

def rmsnorm(x, g):
    xf = x.astype(jnp.float32)
    y = xf * lax.rsqrt(jnp.mean(xf * xf, axis=-1, keepdims=True) + EPS)
    return (y * g.astype(jnp.float32)).astype(x.dtype)

def layernorm(x, g, b):
    xf = x.astype(jnp.float32)
    mu = jnp.mean(xf, axis=-1, keepdims=True)
    xc = xf - mu
    var = jnp.mean(xc * xc, axis=-1, keepdims=True)
    y = xc * lax.rsqrt(var + EPS) * g.astype(jnp.float32) + b.astype(jnp.float32)
    return y.astype(x.dtype)

def _cmul(ar, ai, br, bi):
    return ar * br - ai * bi, ar * bi + ai * br

def _scan_combine(e1, e2):
    a1r, a1i, b1r, b1i = e1
    a2r, a2i, b2r, b2i = e2
    ar, ai = _cmul(a2r, a2i, a1r, a1i)
    br, bi = _cmul(a2r, a2i, b1r, b1i)
    return ar, ai, br + b2r, bi + b2i

def s5_mixer(u, h0_re, h0_im, a_re, a_im, log_dt, b_re, b_im, c_re, c_im, d_skip, w_glu, b_glu):
    bsz, L = u.shape[0], u.shape[1]
    uf = u.astype(jnp.float32)
    dt = jnp.exp(log_dt.astype(jnp.float32))[:, None]
    lam_re = a_re.astype(jnp.float32)
    lam_im = a_im.astype(jnp.float32)
    mag = jnp.exp(lam_re * dt)
    ab_re = mag * jnp.cos(lam_im * dt)
    ab_im = mag * jnp.sin(lam_im * dt)
    den = lam_re * lam_re + lam_im * lam_im
    nr = ab_re - 1.0
    q_re = (nr * lam_re + ab_im * lam_im) / den
    q_im = (ab_im * lam_re - nr * lam_im) / den
    bb_re, bb_im = _cmul(q_re[..., None], q_im[..., None],
                         b_re.astype(jnp.float32), b_im.astype(jnp.float32))
    bu_re = jnp.einsum('blgh,gph->blgp', uf, bb_re)
    bu_im = jnp.einsum('blgh,gph->blgp', uf, bb_im)
    i_re, i_im = _cmul(ab_re, ab_im, h0_re.astype(jnp.float32), h0_im.astype(jnp.float32))
    bu_re = bu_re.at[:, 0].add(i_re)
    bu_im = bu_im.at[:, 0].add(i_im)
    lam_b_re = jnp.broadcast_to(ab_re, bu_re.shape)
    lam_b_im = jnp.broadcast_to(ab_im, bu_im.shape)
    _, _, h_re, h_im = lax.associative_scan(_scan_combine, (lam_b_re, lam_b_im, bu_re, bu_im), axis=1)
    y = (jnp.einsum('blgp,ghp->blgh', h_re, c_re.astype(jnp.float32))
         - jnp.einsum('blgp,ghp->blgh', h_im, c_im.astype(jnp.float32))
         + d_skip.astype(jnp.float32) * uf)
    y = jax.nn.gelu(y)
    z = jnp.einsum('blgh,ghk->blgk', y, w_glu.astype(jnp.float32)) + b_glu.astype(jnp.float32)
    out = z[..., :SSM_GROUP] * jax.nn.sigmoid(z[..., SSM_GROUP:])
    return out.reshape(bsz, L, MIX_A).astype(u.dtype), h_re[:, -1], h_im[:, -1]

def sgu_mixer(u, v, w_s, b_s, ln_g, ln_b):
    bsz, L = u.shape[0], u.shape[1]
    u = jax.nn.gelu(u)
    v = layernorm(jax.nn.gelu(v), ln_g, ln_b)
    c = min(L, CHUNK)
    n = L // c
    mask = jnp.tril(jnp.ones((c, c), dtype=bool))
    ws = jnp.where(mask[None], w_s[:, :c, :c], 0.0)
    vc = v.reshape(bsz, n, c, NH_B, HD_B)
    s = jnp.einsum('hqk,bnkhd->bnqhd', ws, vc) + b_s[:, :c].T[None, None, :, :, None]
    out = u * s.reshape(bsz, L, NH_B, HD_B)
    return out.reshape(bsz, L, MIX_B), v

def swiglu(x, wg, wu, wd):
    return (jax.nn.silu(x @ wg) * (x @ wu)) @ wd

def moe_swiglu(x, w_router, b_router, we_gate, we_up, we_down):
    logits = (x @ w_router).astype(jnp.float32) + b_router.astype(jnp.float32)
    top_v, top_i = lax.top_k(logits, TOP_K)
    top_w = jax.nn.softmax(top_v, axis=-1)
    gates = jnp.sum(jax.nn.one_hot(top_i, N_EXPERTS, dtype=jnp.float32) * top_w[..., None], axis=-2)
    out = jnp.zeros(x.shape, jnp.float32)
    for e in range(N_EXPERTS):
        out = out + gates[..., e:e + 1] * swiglu(x, we_gate[e], we_up[e], we_down[e]).astype(jnp.float32)
    return out.astype(x.dtype)

def _trunk(x, h0_re, h0_im, norm_mix, w_in, ssm_a_re, ssm_a_im, ssm_log_dt, ssm_b_re, ssm_b_im,
           ssm_c_re, ssm_c_im, ssm_d, glu_w, glu_b, sgu_w, sgu_b, sgu_ln_g, sgu_ln_b,
           out_norm_a, out_norm_b, w_out, norm_ffn, ffn_w_gate, ffn_w_up, ffn_w_down,
           router_w, router_b, moe_w_gate, moe_w_up, moe_w_down, norm_final):
    bsz, L = x.shape[0], x.shape[1]
    new_re, new_im, new_v = [], [], []
    for layer in range(DEPTH):
        hn = rmsnorm(x, norm_mix[layer])
        z = hn @ w_in[layer]
        ua = z[..., :MIX_A].reshape(bsz, L, NG_A, SSM_GROUP)
        ub = z[..., MIX_A:MIX_A + MIX_B].reshape(bsz, L, NH_B, HD_B)
        vb = z[..., MIX_A + MIX_B:].reshape(bsz, L, NH_B, HD_B)
        ya, hr, hi = s5_mixer(ua, h0_re[layer], h0_im[layer], ssm_a_re[layer], ssm_a_im[layer],
                              ssm_log_dt[layer], ssm_b_re[layer], ssm_b_im[layer],
                              ssm_c_re[layer], ssm_c_im[layer], ssm_d[layer],
                              glu_w[layer], glu_b[layer])
        yb, vn = sgu_mixer(ub, vb, sgu_w[layer], sgu_b[layer], sgu_ln_g[layer], sgu_ln_b[layer])
        ycat = jnp.concatenate([rmsnorm(ya, out_norm_a[layer]), rmsnorm(yb, out_norm_b[layer])], axis=-1)
        x = x + ycat @ w_out[layer]
        hn2 = rmsnorm(x, norm_ffn[layer])
        if layer % 2 == 0:
            j = layer // 2
            f = swiglu(hn2, ffn_w_gate[j], ffn_w_up[j], ffn_w_down[j])
        else:
            j = layer // 2
            f = moe_swiglu(hn2, router_w[j], router_b[j], moe_w_gate[j], moe_w_up[j], moe_w_down[j])
        x = x + f
        new_re.append(hr)
        new_im.append(hi)
        new_v.append(vn)
    y = rmsnorm(x, norm_final)
    return y, jnp.stack(new_re), jnp.stack(new_im), jnp.stack(new_v)

def setup_inputs(seed: int = 0) -> dict:
    key = jax.random.key(seed)
    ks = jax.random.split(key, 40)
    f32 = jnp.float32
    nrm = lambda k, shape, s: (jax.random.normal(k, shape, f32) * s)
    n_idx = jnp.arange(SSM_STATE, dtype=f32)
    inp = {}
    inp['x_prompt'] = nrm(ks[0], (BATCH, SEQ, D_MODEL), 1.0)
    inp['x_sample'] = nrm(ks[1], (DEC_BATCH, DEC_SEQ, D_MODEL), 1.0)
    inp['state_ssm_re'] = nrm(ks[2], (DEPTH, DEC_BATCH, NG_A, SSM_STATE), 0.5)
    inp['state_ssm_im'] = nrm(ks[3], (DEPTH, DEC_BATCH, NG_A, SSM_STATE), 0.5)
    inp['norm_mix'] = 1.0 + nrm(ks[4], (DEPTH, D_MODEL), 0.02)
    inp['w_in'] = nrm(ks[5], (DEPTH, D_MODEL, IN_WIDTH), D_MODEL ** -0.5)
    inp['ssm_a_re'] = -0.5 + nrm(ks[6], (DEPTH, NG_A, SSM_STATE), 0.01)
    inp['ssm_a_im'] = math.pi * n_idx + nrm(ks[7], (DEPTH, NG_A, SSM_STATE), 0.01)
    inp['ssm_log_dt'] = jax.random.uniform(ks[8], (DEPTH, NG_A), f32, math.log(DT_MIN), math.log(DT_MAX))
    inp['ssm_b_re'] = nrm(ks[9], (DEPTH, NG_A, SSM_STATE, SSM_GROUP), (2 * SSM_GROUP) ** -0.5)
    inp['ssm_b_im'] = nrm(ks[10], (DEPTH, NG_A, SSM_STATE, SSM_GROUP), (2 * SSM_GROUP) ** -0.5)
    inp['ssm_c_re'] = nrm(ks[11], (DEPTH, NG_A, SSM_GROUP, SSM_STATE), (2 * SSM_STATE) ** -0.5)
    inp['ssm_c_im'] = nrm(ks[12], (DEPTH, NG_A, SSM_GROUP, SSM_STATE), (2 * SSM_STATE) ** -0.5)
    inp['ssm_d'] = nrm(ks[13], (DEPTH, NG_A, SSM_GROUP), 1.0)
    inp['glu_w'] = nrm(ks[14], (DEPTH, NG_A, SSM_GROUP, 2 * SSM_GROUP), SSM_GROUP ** -0.5)
    inp['glu_b'] = nrm(ks[15], (DEPTH, NG_A, 2 * SSM_GROUP), 0.02)
    inp['sgu_w'] = nrm(ks[16], (DEPTH, NH_B, CHUNK, CHUNK), CHUNK ** -0.5)
    inp['sgu_b'] = 1.0 + nrm(ks[17], (DEPTH, NH_B, CHUNK), 0.02)
    inp['sgu_ln_g'] = 1.0 + nrm(ks[18], (DEPTH, NH_B, HD_B), 0.02)
    inp['sgu_ln_b'] = nrm(ks[19], (DEPTH, NH_B, HD_B), 0.02)
    inp['out_norm_a'] = 1.0 + nrm(ks[20], (DEPTH, MIX_A), 0.02)
    inp['out_norm_b'] = 1.0 + nrm(ks[21], (DEPTH, MIX_B), 0.02)
    inp['w_out'] = nrm(ks[22], (DEPTH, MIX_WIDTH, D_MODEL), MIX_WIDTH ** -0.5)
    inp['norm_ffn'] = 1.0 + nrm(ks[23], (DEPTH, D_MODEL), 0.02)
    inp['ffn_w_gate'] = nrm(ks[24], (N_DENSE, D_MODEL, D_FF), D_MODEL ** -0.5)
    inp['ffn_w_up'] = nrm(ks[25], (N_DENSE, D_MODEL, D_FF), D_MODEL ** -0.5)
    inp['ffn_w_down'] = nrm(ks[26], (N_DENSE, D_FF, D_MODEL), D_FF ** -0.5)
    inp['router_w'] = nrm(ks[27], (N_MOE, D_MODEL, N_EXPERTS), D_MODEL ** -0.5)
    inp['router_b'] = nrm(ks[28], (N_MOE, N_EXPERTS), 0.01)
    inp['moe_w_gate'] = nrm(ks[29], (N_MOE, N_EXPERTS, D_MODEL, D_FF_EXPERT), D_MODEL ** -0.5)
    inp['moe_w_up'] = nrm(ks[30], (N_MOE, N_EXPERTS, D_MODEL, D_FF_EXPERT), D_MODEL ** -0.5)
    inp['moe_w_down'] = nrm(ks[31], (N_MOE, N_EXPERTS, D_FF_EXPERT, D_MODEL), D_FF_EXPERT ** -0.5)
    inp['norm_final'] = 1.0 + nrm(ks[32], (D_MODEL,), 0.02)
    return inp

def reference(x_prompt, x_sample, state_ssm_re, state_ssm_im, norm_mix, w_in, ssm_a_re, ssm_a_im,
              ssm_log_dt, ssm_b_re, ssm_b_im, ssm_c_re, ssm_c_im, ssm_d, glu_w, glu_b, sgu_w, sgu_b,
              sgu_ln_g, sgu_ln_b, out_norm_a, out_norm_b, w_out, norm_ffn, ffn_w_gate, ffn_w_up,
              ffn_w_down, router_w, router_b, moe_w_gate, moe_w_up, moe_w_down, norm_final):
    weights = (norm_mix, w_in, ssm_a_re, ssm_a_im, ssm_log_dt, ssm_b_re, ssm_b_im, ssm_c_re, ssm_c_im,
               ssm_d, glu_w, glu_b, sgu_w, sgu_b, sgu_ln_g, sgu_ln_b, out_norm_a, out_norm_b, w_out,
               norm_ffn, ffn_w_gate, ffn_w_up, ffn_w_down, router_w, router_b, moe_w_gate, moe_w_up,
               moe_w_down, norm_final)
    h0 = jnp.zeros((DEPTH, x_prompt.shape[0], NG_A, SSM_STATE), jnp.float32)
    y_prompt, ssm_re_prompt, ssm_im_prompt, _ = _trunk(x_prompt, h0, h0, *weights)
    y_sample, ssm_re_sample, ssm_im_sample, sgu_v_sample = _trunk(x_sample, state_ssm_re, state_ssm_im, *weights)
    return (y_prompt, y_sample, ssm_re_prompt, ssm_im_prompt, ssm_re_sample, ssm_im_sample, sgu_v_sample)


_drawn_inputs = setup_inputs


def setup_inputs(seed=0):
    import zlib

    import numpy as np

    out = dict(_drawn_inputs(seed))
    spreads = {}
    factors = {'ssm_a_re': 63.54,
     'sgu_ln_g': 8.311,
     'sgu_ln_b': 8.06,
     'router_b': 4.583,
     'norm_final': 20.478,
     'sgu_b': 2.677}
    for name, (base, spread) in spreads.items():
        noise = np.random.default_rng([zlib.crc32(name.encode()), seed]).standard_normal(out[name].shape)
        drawn = base * np.exp(spread * noise) if base else spread * noise
        out[name] = __import__('jax').numpy.asarray(drawn.astype(out[name].dtype))
    for name, factor in factors.items():
        out[name] = (out[name] * factor).astype(out[name].dtype)
    return out
```

```python
from contextlib import ExitStack

import numpy as np

import concourse.bass as bass
from concourse import mybir

F32 = mybir.dt.float32
I32 = mybir.dt.int32
U32 = mybir.dt.uint32
ALU = mybir.AluOpType
ACT = mybir.ActivationFunctionType
AX = mybir.AxisListType

P = 128
DEPTH = 2
DM = 1024
KT = DM // P
BS, LS = 8, 4
NSAMP = BS * LS
NPROMPT = 256
T = NSAMP + NPROMPT
CH = 4
NCS = NSAMP // CH
NCP = NPROMPT // CH
NCH = NCS + NCP
TILES = [(0, NSAMP), (NSAMP, P), (NSAMP + P, P)]
MIX = DM // 2
MT = MIX // P
IN_W = 3 * MIX
NG, GH, NST = 32, 16, 64
NP = NG // 2
NH, HD = 8, 64
QC = 128
FF = 1376
FT = 11
NE = 8
EPS = 1e-6
PIECES = 4
DPIECE = [(0, 3), (3, 6), (6, 9), (9, 11)]
FCH = [(0, 512), (512, 1024), (1024, FF)]
MAXPASS = 3
TAB = MAXPASS * NE + 1
TWO_PI = 6.283185307179586
C1 = 6.28125
C2 = TWO_PI - C1
ROUND = 12582912.0
PI_SAFE = 3.1415925

COLS = {}
_at = 0
for _name, _n in [("norm_mix", 8), ("out_norm_a", 4), ("out_norm_b", 4), ("norm_ffn", 8),
                  ("glu_b1", 4), ("glu_b2", 4), ("ssm_d", 4), ("a_re", 16), ("a_im", 16),
                  ("log_dt", 16)]:
    COLS[_name] = (_at, _n)
    _at += _n
NCOL = _at

X_OUT = [0, 24]
X_DENSE = [8, 16]
X_MOE = 32


def bc(ap, n):
    return ap.unsqueeze(2).to_broadcast([ap.shape[0], ap.shape[1], n])


def rows(kk):
    return P if kk < FT - 1 else FF - P * (FT - 1)


def build(nc, x_d, consts_d, cols_d, misc_d, w_in_d, w_out_d, b_d, c_d, glu_d, ln_d, wst_d, wss_d,
          sbias_d, h0_d, ffn_g_d, ffn_u_d, ffn_d_d, moe_g_d, moe_u_d, moe_d_d,
          y_d, sp_d, ss_d, vn_d):
    ctx = ExitStack()
    with ctx:
        def sb(name, n, dt=F32):
            return ctx.enter_context(nc.sbuf_tensor(name, [P, n], dt))

        def sem(name):
            return ctx.enter_context(nc.semaphore(name))

        G = sb("G", KT * IN_W)
        U = sb("U", KT * FF)
        D = sb("D", FT * DM)
        M = sb("M", 10272)
        xb = sb("xb", KT * T)
        hb = sb("hb", KT * T)
        consts = sb("consts", 5 * P)
        cols = sb("cols", DEPTH * NCOL + 8)
        misc = sb("misc", 72)
        sbias = sb("sbias", NH * (LS + QC))
        wss = sb("wss", NH * NSAMP)
        rs = sb("rs", 2 * T)
        sg = sb("sg", 2 * T)
        fin = sb("fin", 2 * NP * NCS)
        finp = sb("finp", 2 * NP)
        a4 = sb("a4", 2 * NP)
        hb2 = sb("hb2", DEPTH * 4)
        eps = sb("eps", 1)
        ni_sb = sb("ni_sb", 1, I32)

        x = xb[:, :].rearrange("p (k t) -> p k t", t=T)
        h = hb[:, :].rearrange("p (k t) -> p k t", t=T)
        ident = consts[:, 0:P]
        upper = consts[:, P:2 * P]
        strict = consts[:, 2 * P:3 * P]
        iota = consts[:, 3 * P:4 * P]
        ones = consts[:, 4 * P:5 * P]
        rw = misc[:, 0:64].rearrange("p (k e) -> p k e", e=NE)
        rb = misc[:, 64:72]
        sbr = sbias[0:1, :].rearrange("p (h t) -> p h t", h=NH)
        wssv = wss[0:NSAMP, :].rearrange("p (h t) -> p h t", h=NH)

        def col(l, name, i=0, n=1):
            return cols[:, l * NCOL + COLS[name][0] + i:l * NCOL + COLS[name][0] + i + n]

        w_in = G[:, :].rearrange("p (k f) -> p k f", f=IN_W)
        gate = G[:, 0:KT * FF].rearrange("p (k f) -> p k f", f=FF)
        up = U[:, :].rearrange("p (k f) -> p k f", f=FF)
        down = D[:, :].rearrange("p (k f) -> p k f", f=DM)
        w_out = D[:, 0:KT * DM].rearrange("p (k f) -> p k f", f=DM)
        BT = U[:, 0:4096].rearrange("p (q r j s) -> p q r j s", q=MT, r=2, j=CH)
        CPX = U[:, 4096:9216].rearrange("p (r n s f) -> p r n s f", r=2, n=NP, s=CH + 1)
        mag_tab = U[:, 9216:10240].rearrange("p (n c) -> p n c", n=NP)
        wr = U[:, 10240:10496]
        wi = U[:, 10496:10752]
        tmp = U[:, 10752:11008]
        lt = U[:, 10240:10752]
        mu = U[:, 10752:10776]
        var = U[:, 10776:10800]
        nwt = U[:, 10800:10848]
        BPX = D[:, 0:4096].rearrange("p (r s n f) -> p r s n f", r=2, s=CH, n=NP)
        bt1 = D[:, 4096:4608].rearrange("p (n f) -> p n f", n=NP)
        bt2 = D[:, 4608:5120].rearrange("p (n f) -> p n f", n=NP)
        ct1 = D[:, 5120:5632].rearrange("p (n f) -> p n f", n=NP)
        ct2 = D[:, 5632:6144].rearrange("p (n f) -> p n f", n=NP)
        rt1 = D[:, 6144:6656]
        rt2 = D[:, 6656:7168]

        def sv(i, n=1):
            return D[:, 7168 + 16 * i:7168 + 16 * (i + n)]

        glu = D[:, 8192:9216].rearrange("p (q z f) -> p q z f", q=MT, z=2)
        lng = D[:, 9216:9728]
        lnb = D[:, 9728:10240]
        wst = D[:, 10240:11264].rearrange("p (h q) -> p h q", h=NH)
        Kt = M[:, 0:2048].rearrange("p (q s f) -> p q s f", q=MT, s=CH)
        rot = M[:, 2048:4096].rearrange("p (r n c) -> p r n c", r=2, n=NP)
        S = M[:, 4096:6432].rearrange("p (r n c) -> p r n c", r=2, n=NP)
        ua = M[:, 6432:7584].rearrange("p (q t) -> p q t", q=MT)
        ub = M[:, 7584:8736].rearrange("p (q t) -> p q t", q=MT)
        v = M[:, 8736:10272].rearrange("p (t f) -> p t f", t=3)
        sq2 = M[:, 0:KT * T].rearrange("p (k t) -> p k t", t=T)
        hid = M[:, 4096:4096 + FT * T].rearrange("p (m t) -> p m t", t=T)
        h_tok = M[:, 2304:5376].rearrange("p (t f) -> p t f", t=3)
        hg = M[:, 5376:6400].rearrange("p (k s) -> p k s", k=KT)
        sge = M[:, 0:FF]
        he = M[:, 6400:7776]
        het = M[:, 7776:9184].rearrange("p (k s) -> p k s", k=FT)
        ye = M[:, 9184:10208]
        oh = M[:, 1376:1760].rearrange("p (t s) -> p t s", t=3)
        goh = M[:, 1760:2144].rearrange("p (t s) -> p t s", t=3)
        sgt = sg[:, 0:T]
        small = G[:, 11008:11168]
        lg = small[:, 0:24].rearrange("p (t e) -> p t e", t=3)
        m8 = small[:, 24:48].rearrange("p (t e) -> p t e", t=3)
        ixf = small[:, 48:72].rearrange("p (t e) -> p t e", t=3)
        mask = small[:, 72:96].rearrange("p (t e) -> p t e", t=3)
        gts = small[:, 96:120].rearrange("p (t e) -> p t e", t=3)
        e1 = small[:, 120:123]
        w0 = small[:, 123:126]
        w1 = small[:, 126:129]
        cn = small[:, 129:132]
        r8 = small[:, 136:160].rearrange("p (t e) -> p t e", t=3)
        ixv = G[:, 11168:11192].bitcast(U32).rearrange("p (t e) -> p t e", t=3)
        postab = G[:, 11192:11192 + 3 * TAB]
        gatetab = G[:, 11272:11272 + 3 * TAB]
        pos = postab[:, :].rearrange("p (t i) -> p t i", t=3)
        gat = gatetab[:, :].rearrange("p (t i) -> p t i", t=3)

        ps = ctx.enter_context(nc.psum_tensor("ps", [P, 8, 512], F32))

        def bank(b, n=T, at=0):
            return ps[:, b, at:at + n]

        x_in = sem("x_in")
        const_in = sem("const_in")
        prep_in = sem("prep_in")
        mix_in = sem("mix_in")
        g_in = [sem(f"g_in{j}") for j in range(PIECES)]
        u_in = [sem(f"u_in{j}") for j in range(PIECES)]
        d_in = [sem(f"d_in{j}") for j in range(PIECES)]
        out_done = sem("out_done")
        fin_out = sem("fin_out")
        vn_out = sem("vn_out")
        gate_used = sem("gate_used")
        up_used = sem("up_used")
        down_used = sem("down_used")
        sq_ready = sem("sq_ready")
        ms_mm = sem("ms_mm")
        sd_ready = sem("sd_ready")
        h_ready = sem("h_ready")
        xadd = sem("xadd")
        dt_ready = sem("dt_ready")
        th_ready = sem("th_ready")
        mag_ready = sem("mag_ready")
        ang_ready = sem("ang_ready")
        trig_ready = sem("trig_ready")
        a_ready = sem("a_ready")
        bp_ready = sem("bp_ready")
        cp_ready = sem("cp_ready")
        rot_ready = sem("rot_ready")
        set_ready = sem("set_ready")
        bt_mm = sem("bt_mm")
        bt_ready = sem("bt_ready")
        ua_mm = sem("ua_mm")
        ua_ready = sem("ua_ready")
        v_mm = sem("v_mm")
        v_ready = sem("v_ready")
        vn_ready = sem("vn_ready")
        ub_mm = sem("ub_mm")
        ub_ready = sem("ub_ready")
        s_mm = sem("s_mm")
        s_used = sem("s_used")
        st_ready = sem("st_ready")
        fin_ready = sem("fin_ready")
        k_mm = sem("k_mm")
        k_ready = sem("k_ready")
        y_mm = sem("y_mm")
        y_ready = sem("y_ready")
        sgu_mm = sem("sgu_mm")
        yb_ready = sem("yb_ready")
        wst_ready = sem("wst_ready")
        glu_mm = sem("glu_mm")
        th2_ready = sem("th2_ready")
        ya_ready = sem("ya_ready")
        wo_mm = sem("wo_mm")
        gu_mm = sem("gu_mm")
        silu_ready = sem("silu_ready")
        hid_ready = sem("hid_ready")
        dn_mm = sem("dn_mm")
        small = G[:, 11008:11168]
        lg_mm = sem("lg_mm")
        htok_mm = sem("htok_mm")
        htok_ready = sem("htok_ready")
        d_ready = sem("d_ready")
        e_ready = sem("e_ready")
        mask_ready = sem("mask_ready")
        pos_mm = sem("pos_mm")
        ni_ready = sem("ni_ready")
        oh_ready = sem("oh_ready")
        gtr_mm = sem("gtr_mm")
        sgt_ready = sem("sgt_ready")
        gather_mm = sem("gather_mm")
        hg_ready = sem("hg_ready")
        egu_mm = sem("egu_mm")
        esilu_ready = sem("esilu_ready")
        he_ready = sem("he_ready")
        etr_mm = sem("etr_mm")
        het_ready = sem("het_ready")
        ed_mm = sem("ed_mm")
        ye_ready = sem("ye_ready")
        sc_mm = sem("sc_mm")
        dve_chain = sem("dve_chain")
        act_chain = sem("act_chain")
        pool_chain = sem("pool_chain")

        moe_g = moe_g_d.rearrange("e (k p) f -> e p k f", p=P)
        moe_u = moe_u_d.rearrange("e (k p) f -> e p k f", p=P)

        block = ctx.enter_context(nc.Block())

        @block.sync
        def _(sp):
            sp.dma_start(x, x_d).then_inc(x_in, 16)

            def load_in(l):
                src = w_in_d[l].rearrange("(k p) f -> p k f", p=P)
                for j in range(PIECES):
                    sp.dma_start(w_in[:, 2 * j:2 * j + 2, :], src[:, 2 * j:2 * j + 2, :]).then_inc(g_in[j], 16)

            def load_out(l):
                src = w_out_d[l].rearrange("(k p) f -> p k f", p=P)
                for j in range(PIECES):
                    sp.dma_start(w_out[:, 2 * j:2 * j + 2, :], src[:, 2 * j:2 * j + 2, :]).then_inc(d_in[j], 16)

            def load_cols(dst, src, sems, free):
                for j in range(PIECES):
                    if free:
                        sp.wait_ge(*free[j])
                    sp.dma_start(dst[:, 2 * j:2 * j + 2, :], src[:, 2 * j:2 * j + 2, :]).then_inc(sems[j], 16)

            def load_down(src, free):
                for j, (a, b) in enumerate(DPIECE):
                    if free:
                        sp.wait_ge(*free[j])
                    full = min(b, FT - 1)
                    last = b == FT
                    sp.dma_start(down[:, a:full, :],
                                 src[a * P:full * P, :].rearrange("(k p) f -> p k f", p=P)).then_inc(d_in[j], 16)
                    if last:
                        sp.dma_start(down[0:rows(FT - 1), FT - 1, :], src[(FT - 1) * P:FF, :]).then_inc(d_in[j], 16)

            load_in(0)
            for l in range(DEPTH):
                sp.wait_ge(bt_mm, 8 * (l + 1))
                sp.wait_ge(k_mm, l + 1)
                sp.wait_ge(cp_ready, l + 1)
                sp.wait_ge(rot_ready, l + 1)
                load_out(l)
                if l == 0:
                    for hf in range(2):
                        f0 = hf * FF
                        g_src = ffn_g_d[0, :, f0:f0 + FF].rearrange("(k p) f -> p k f", p=P)
                        u_src = ffn_u_d[0, :, f0:f0 + FF].rearrange("(k p) f -> p k f", p=P)
                        if hf == 0:
                            sp.wait_ge(ub_mm, 4)
                            load_cols(gate, g_src, g_in, None)
                            sp.wait_ge(y_mm, 4)
                            load_cols(up, u_src, u_in, None)
                            sp.wait_ge(wo_mm, 8)
                        else:
                            load_cols(gate, g_src, g_in, [(gate_used, j + 1) for j in range(PIECES)])
                            load_cols(up, u_src, u_in, [(up_used, 1), (up_used, 2), (up_used, 3), (gu_mm, FT)])
                        load_down(ffn_d_d[0, f0:f0 + FF, :], hf and
                                  [(down_used, 1), (down_used, 2), (down_used, 3), (dn_mm, KT)])
                    sp.wait_ge(gate_used, 8)
                    load_in(1)
                else:
                    sp.wait_ge(ub_mm, 8)
                    load_cols(gate, moe_g[0], g_in, None)
                    sp.wait_ge(y_mm, 8)
                    load_cols(up, moe_u[0], u_in, None)
                    sp.wait_ge(wo_mm, 16)
                    load_down(moe_d_d[0], None)
            sp.wait_ge(ni_ready, 1)
            turns = sp.value_load(ni_sb[0:1, 0:1], min_val=NE, max_val=MAXPASS * NE)
            with sp.Fori(1, turns) as i:
                e = i % NE
                for j in range(PIECES):
                    sp.wait_ge(gate_used, 4 * i + (4 + j + 1))
                    sp.dma_start(gate[:, 2 * j:2 * j + 2, :], moe_g[e, :, 2 * j:2 * j + 2, :]).then_inc(g_in[j], 16)
                    if j < PIECES - 1:
                        sp.wait_ge(up_used, 3 * i + (3 + j + 1))
                    else:
                        sp.wait_ge(egu_mm, 3 * i)
                    sp.dma_start(up[:, 2 * j:2 * j + 2, :], moe_u[e, :, 2 * j:2 * j + 2, :]).then_inc(u_in[j], 16)
                load_down(moe_d_d[e], [(down_used, 3 * i + (3 + j + 1)) for j in range(PIECES - 1)] + [(ed_mm, i)])
            for k in range(KT):
                sp.wait_ge(h_ready, 48 + k + 1)
                sp.dma_start(y_d[:, k, :], h[:, k, :]).then_inc(out_done, 16)
            sp.wait_ge(out_done, 16 * KT)

        @block.gpsimd
        def _(pool):
            n_chain = [0]

            def link(ins):
                n_chain[0] += 1
                ins.then_inc(pool_chain, 1)
                pool.wait_ge(pool_chain, n_chain[0])

            pool.dma_start(cols[:, :], cols_d).then_inc(const_in, 16)
            pool.dma_start(consts[:, :], consts_d).then_inc(const_in, 16)
            pool.dma_start(misc[:, :], misc_d).then_inc(const_in, 16)
            for l in range(DEPTH):
                if l:
                    pool.wait_ge(dn_mm, 16)
                pool.dma_start(BPX[:, :, 0, :, :], b_d[l]).then_inc(prep_in, 16)
                for r in range(2):
                    pool.dma_start(CPX[:, r, :, 0, :], c_d[l, :, r]).then_inc(prep_in, 16)
                pool.dma_start(glu, glu_d[l]).then_inc(mix_in, 16)
                pool.dma_start(D[:, 9216:10240], ln_d[l]).then_inc(mix_in, 16)
                pool.dma_start(wst, wst_d[l]).then_inc(mix_in, 16)
                pool.dma_start(wss[0:NSAMP, :], wss_d[l]).then_inc(mix_in, 16)
                pool.dma_start(sbias[0:1, :], sbias_d[l:l + 1, :]).then_inc(mix_in, 16)
                for r in range(2):
                    pool.dma_start(S[:, r, :, 0:NCS], h0_d[l, :, r]).then_inc(mix_in, 16)
                pool.memset(M[:, 0:2048], 0.0).then_inc(set_ready, 1)
                pool.memset(S[:, :, :, NCS:NCS + 1], 0.0).then_inc(set_ready, 1)
                pool.wait_ge(const_in, 48)
                pool.wait_ge(mix_in, 112 * (l + 1))
                up_b = upper.unsqueeze(1).to_broadcast([P, NH, QC])
                pool.tensor_tensor(wst, wst, up_b, ALU.mult).then_inc(wst_ready, 1)
                up_s = upper[0:NSAMP, 0:NSAMP].unsqueeze(1).to_broadcast([NSAMP, NH, NSAMP])
                pool.tensor_tensor(wssv, wssv, up_s, ALU.mult).then_inc(wst_ready, 1)
                pool.wait_ge(prep_in, 48 * (l + 1))
                link(pool.tensor_scalar(CPX[:, 1, :, 0, :], CPX[:, 1, :, 0, :], -1.0, None, ALU.mult))
                pool.wait_ge(a_ready, l + 1)
                ar, ai = bc(sv(10), 32), bc(sv(11), 32)
                for s in range(CH):
                    re, ni = CPX[:, 0, :, s, :], CPX[:, 1, :, s, :]
                    re1, ni1 = CPX[:, 0, :, s + 1, :], CPX[:, 1, :, s + 1, :]
                    pool.tensor_tensor(ct1, ai, ni, ALU.mult)
                    pool.tensor_tensor(ct2, ai, re, ALU.mult)
                    pool.tensor_tensor(re1, ar, re, ALU.mult)
                    link(pool.tensor_tensor(ni1, ar, ni, ALU.mult))
                    pool.tensor_tensor(re1, re1, ct1, ALU.add)
                    last = pool.tensor_tensor(ni1, ni1, ct2, ALU.subtract)
                    if s < CH - 1:
                        link(last)
                    else:
                        last.then_inc(cp_ready, 1)
                er, ei = sv(12), sv(13)
                pool.memset(rot[:, 0, :, 0:1], 1.0)
                link(pool.memset(rot[:, 1, :, 0:1], 0.0))
                n = 1
                while n < NCP:
                    lo_r, lo_i = rot[:, 0, :, 0:n], rot[:, 1, :, 0:n]
                    hi_r, hi_i = rot[:, 0, :, n:2 * n], rot[:, 1, :, n:2 * n]
                    t1 = rt1[:, 0:NP * n].rearrange("p (a b) -> p a b", b=n)
                    t2 = rt2[:, 0:NP * n].rearrange("p (a b) -> p a b", b=n)
                    pool.tensor_tensor(t1, bc(ei, n), lo_i, ALU.mult)
                    pool.tensor_tensor(t2, bc(ei, n), lo_r, ALU.mult)
                    pool.tensor_tensor(hi_r, bc(er, n), lo_r, ALU.mult)
                    link(pool.tensor_tensor(hi_i, bc(er, n), lo_i, ALU.mult))
                    pool.tensor_tensor(hi_r, hi_r, t1, ALU.subtract)
                    last = pool.tensor_tensor(hi_i, hi_i, t2, ALU.add)
                    n *= 2
                    if n == NCP:
                        last.then_inc(rot_ready, 1)
                        break
                    link(last)
                    pool.tensor_tensor(sv(14), er, er, ALU.mult)
                    pool.tensor_tensor(sv(15), ei, ei, ALU.mult)
                    link(pool.tensor_tensor(sv(16), er, ei, ALU.mult))
                    pool.tensor_tensor(er, sv(14), sv(15), ALU.subtract)
                    link(pool.tensor_tensor(ei, sv(16), sv(16), ALU.add))
                pool.wait_ge(vn_ready, 3 * l + 1)
                pool.dma_start(vn_d[l], v[0:NSAMP, 0, :]).then_inc(vn_out, 16)
                pool.wait_ge(fin_ready, l + 1)
                pool.dma_start(ss_d[l], fin[:, :]).then_inc(fin_out, 16)
                pool.dma_start(sp_d[l], finp[:, :]).then_inc(fin_out, 16)
            pool.wait_ge(fin_out, 32 * DEPTH)
            pool.wait_ge(vn_out, 16 * DEPTH)

        @block.scalar
        def _(act):
            def squares(src, dst, k0, wait):
                for k in range(src.shape[1]):
                    wait(k)
                    act.activation(dst[:, k0 + k, :], src[:, k, :], ACT.Square).then_inc(sq_ready, 1)

            def root(n, b, width, slot):
                act.wait_ge(ms_mm, n + 1)
                act.activation(rs[:, slot * T:(slot + 1) * T], bank(b), ACT.Sqrt, bias=eps[:, 0:1],
                               scale=1.0 / width).then_inc(sd_ready, 1)

            act.wait_ge(dve_chain, 1)
            for l in range(DEPTH):
                if l == 0:
                    act.wait_ge(x_in, 16)
                    squares(x, h, 0, lambda k: None)
                else:
                    squares(x, h, 0, lambda k: act.wait_ge(xadd, X_DENSE[1] + k + 1))
                root(4 * l, 0, DM, 0)
                act.wait_ge(const_in, 48)
                if l:
                    act.wait_ge(dn_mm, 16)
                act.activation(sv(0), col(l, "log_dt", 0, 16), ACT.Exp).then_inc(dt_ready, 1)
                act.wait_ge(th_ready, l + 1)
                act.activation(sv(3), sv(1), ACT.Exp)
                act.activation(sv(4), sv(1), ACT.Exp, scale=float(CH)).then_inc(mag_ready, 1)
                act.wait_ge(ang_ready, l + 1)
                act.activation(sv(7), sv(5), ACT.Sin)
                act.activation(sv(8), sv(6), ACT.Sin).then_inc(trig_ready, 1)
                for q in range(MT):
                    act.wait_ge(ua_mm, 4 * l + q + 1)
                    act.activation(ua[:, q, :], bank(q), ACT.Copy).then_inc(ua_ready, 1)
                if l:
                    act.wait_ge(vn_out, 16)
                for t, (_, n) in enumerate(TILES):
                    act.wait_ge(v_mm, 3 * l + t + 1)
                    act.activation(v[0:n, t, :], ps[0:n, t, :], ACT.Gelu_apprx_tanh).then_inc(v_ready, 1)
                for n in range(2 * CH):
                    r, s = n // CH, n % CH
                    act.wait_ge(bt_mm, 8 * l + n + 1)
                    act.activation(BT[:, :, r, CH - 1 - s, :],
                                   ps[:, n % 4, :].rearrange("p (q s) -> p q s", q=MT),
                                   ACT.Copy).then_inc(bt_ready, 1)
                for q in range(MT):
                    act.wait_ge(ub_mm, 4 * l + q + 1)
                    act.activation(ub[:, q, :], bank(q), ACT.Gelu_apprx_tanh).then_inc(ub_ready, 1)
                for q in range(MT):
                    act.wait_ge(y_mm, 4 * l + q + 1)
                    act.activation(ua[:, q, :], bank((q + 1) % 4), ACT.Gelu_apprx_tanh).then_inc(y_ready, 1)
                for q in range(MT):
                    act.wait_ge(glu_mm, 4 * l + q + 1)
                    if q >= 2:
                        act.wait_ge(ya_ready, 4 * l + q - 1)
                    act.activation(sg[:, (q % 2) * T:(q % 2 + 1) * T], bank(2 if q % 2 == 0 else 0),
                                   ACT.Tanh, bias=hb2[:, 4 * l + q:4 * l + q + 1],
                                   scale=0.5).then_inc(th2_ready, 1)
                squares(ub, h, MT, lambda k: act.wait_ge(yb_ready, 4 * l + k + 1))
                squares(ua, h, 0, lambda k: act.wait_ge(ya_ready, 4 * l + k + 1))
                root(4 * l + 1, 4, MIX, 1)
                root(4 * l + 2, 5, MIX, 0)
                squares(x, sq2, 0, lambda k: act.wait_ge(xadd, X_OUT[l] + k + 1))
                root(4 * l + 3, 6, DM, 0)
                if l == 0:
                    for n in range(2 * FT):
                        m = n % FT
                        act.wait_ge(gu_mm, n + 1)
                        if n >= 2:
                            act.wait_ge(hid_ready, n - 1)
                        r = rows(m)
                        act.activation(sg[0:r, (n % 2) * T:(n % 2 + 1) * T], ps[0:r, 2 * (m % 4), 0:T],
                                       ACT.Silu).then_inc(silu_ready, 1)
            act.wait_ge(vn_out, 32)
            for n in range(6):
                t = n // 2
                act.wait_ge(htok_mm, n + 1)
                act.activation(h_tok[0:TILES[t][1], t, (n % 2) * 512:(n % 2 + 1) * 512],
                               ps[0:TILES[t][1], n + 1, :], ACT.Copy).then_inc(htok_ready, 1)
            act.wait_ge(d_ready, 1)
            act.activation(e1, cn, ACT.Exp).then_inc(e_ready, 1)
            act.wait_ge(ni_ready, 1)
            turns = act.value_load(ni_sb[0:1, 0:1], min_val=NE, max_val=MAXPASS * NE)
            with act.Fori(0, turns) as i:
                for b in range(2):
                    act.wait_ge(gather_mm, 2 * i + (b + 1))
                    act.activation(hg[:, 4 * b:4 * b + 4, :],
                                   ps[:, 6 + b, :].rearrange("p (k s) -> p k s", s=P),
                                   ACT.Copy).then_inc(hg_ready, 1)
                for c, (a, b) in enumerate(FCH):
                    act.wait_ge(egu_mm, 3 * i + (c + 1))
                    act.activation(sge[:, a:b], ps[:, c, 0:b - a], ACT.Silu).then_inc(esilu_ready, 1)
                for c in range(3):
                    act.wait_ge(etr_mm, 3 * i + (c + 1))
                    n = 4 if c < 2 else 2
                    act.activation(het[:, 4 * c:4 * c + n, :],
                                   ps[:, c, 0:n * P].rearrange("p (k s) -> p k s", s=P),
                                   ACT.Copy).then_inc(het_ready, 1)
                r = rows(FT - 1)
                act.activation(het[0:r, FT - 1, :], ps[0:r, 2, 2 * P:3 * P], ACT.Copy).then_inc(het_ready, 1)
                act.wait_ge(ed_mm, i + 1)
                for b in range(2):
                    act.activation(ye[:, 512 * b:512 * b + 512], ps[:, 6 + b, :], ACT.Copy).then_inc(ye_ready, 1)
            act.wait_ge(xadd, 8 * turns + X_MOE)
            squares(x, h, 0, lambda k: None)
            root(8, 7, DM, 0)

        @block.tensor
        def _(pe):
            def mean_sum(src, k0, n, b, need):
                for k in range(n):
                    pe.wait_ge(sq_ready, need + k + 1)
                    mm = pe.matmul(bank(b), ones, src[:, k0 + k, :], start=(k == 0), stop=(k == n - 1))
                mm.then_inc(ms_mm, 1)

            def weights_here(sems, n):
                for s in sems:
                    pe.wait_ge(s, 16 * n)

            pe.wait_ge(const_in, 48)
            for l in range(DEPTH):
                mean_sum(h, 0, KT, 0, 24 * l)
                for q in range(MT):
                    for k in range(KT):
                        if q == 0:
                            pe.wait_ge(h_ready, 24 * l + k + 1)
                            pe.wait_ge(g_in[k // 2], 16 * (3 * l + 1))
                        mm = pe.matmul(bank(q), w_in[:, k, q * P:(q + 1) * P], h[:, k, :],
                                       start=(k == 0), stop=(k == KT - 1))
                    mm.then_inc(ua_mm, 1)
                for t, (t0, n) in enumerate(TILES):
                    pe.wait_ge(ua_ready, 4 * l + t + 1)
                    for k in range(KT):
                        mm = pe.matmul(ps[0:n, t, :], h[:, k, t0:t0 + n], w_in[:, k, 2 * MIX:IN_W],
                                       start=(k == 0), stop=(k == KT - 1))
                    mm.then_inc(v_mm, 1)
                pe.wait_ge(bp_ready, l + 1)
                for n in range(2 * CH):
                    r, s = n // CH, n % CH
                    if n < 3:
                        pe.wait_ge(v_ready, 3 * l + n + 1)
                    elif n == 3:
                        pe.wait_ge(ua_ready, 4 * l + 4)
                    else:
                        pe.wait_ge(bt_ready, 8 * l + n - 3)
                    for q in range(MT):
                        mm = pe.transpose(bank(n % 4, P, q * P), BPX[:, r, s, 4 * q:4 * q + 4, :], ident)
                    mm.then_inc(bt_mm, 1)
                pe.wait_ge(bt_ready, 8 * (l + 1))
                for q in range(MT):
                    if q >= 2:
                        pe.wait_ge(s_used, 4 * l + q - 1)
                    uv = ua[:, q, :].rearrange("p (c j) -> p c j", j=CH)
                    for r in range(2):
                        for j in range(CH):
                            for pp in range(4):
                                a, b = 32 * pp, 32 * pp + 32
                                mm = pe.matmul(bank(4 * ((q + 1) % 2) + pp, NCH, r * NCH),
                                               BT[a:b, q, r, j, :], uv[a:b, :, j],
                                               start=(j == 0), stop=(j == CH - 1))
                    mm.then_inc(s_mm, 1)
                for q in range(MT):
                    pe.wait_ge(s_used, 4 * (l + 1))
                    for k in range(KT):
                        mm = pe.matmul(bank(q), w_in[:, k, MIX + q * P:MIX + (q + 1) * P], h[:, k, :],
                                       start=(k == 0), stop=(k == KT - 1))
                    mm.then_inc(ub_mm, 1)
                pe.wait_ge(cp_ready, l + 1)
                pe.wait_ge(ub_ready, 4 * l + 1)
                for q in range(MT):
                    for pp in range(4):
                        for r in range(2):
                            mm = pe.matmul(ps[32 * pp:32 * pp + 32, 0, q * P:(q + 1) * P],
                                           BPX[:, r, 0, 4 * q + pp, :], CPX[:, r, 4 * q + pp, 0:CH, :],
                                           start=(r == 0), stop=(r == 1))
                mm.then_inc(k_mm, 1)
                pe.wait_ge(k_ready, l + 1)
                for q in range(MT):
                    pe.wait_ge(ub_ready, 4 * l + min(q + 2, 4))
                    pe.wait_ge(st_ready, 4 * l + q + 1)
                    b = (q + 1) % 4
                    uv = ua[:, q, :].rearrange("p (c j) -> p c j", j=CH)
                    yv = bank(b).rearrange("p (c j) -> p c j", j=CH)
                    for s in range(CH):
                        pe.matmul(yv[:, :, s:CH], Kt[:, q, s, :], uv[:, :, 0:CH - s],
                                  start=(s == 0), stop=False, skip_group_check=True)
                    for r in range(2):
                        for j in range(CH):
                            for pp in range(4):
                                n = 4 * q + pp
                                mm = pe.matmul(yv[32 * pp:32 * pp + 32, :, j], CPX[:, r, n, j + 1, :],
                                               S[:, r, n, 0:NCH], start=False,
                                               stop=(r == 1), skip_group_check=True)
                    mm.then_inc(y_mm, 1)
                pe.wait_ge(mix_in, 112 * (l + 1))
                pe.wait_ge(wst_ready, 2 * (l + 1))
                pe.wait_ge(vn_ready, 3 * (l + 1))
                pe.wait_ge(s_used, 4 * (l + 1))
                for ft in range(MT):
                    for hh in range(2):
                        hd = 2 * ft + hh
                        o = ps[64 * hh:64 * hh + 64, 4 + ft, :]
                        pe.matmul(o[:, 0:NSAMP].rearrange("p (b j) -> p b j", j=LS), ones[0:1, 0:HD],
                                  sbr[:, hd, 0:LS].unsqueeze(1).to_broadcast([1, BS, LS]),
                                  start=True, stop=False, skip_group_check=True)
                        pe.matmul(o[:, NSAMP:T].rearrange("p (b j) -> p b j", j=QC), ones[0:1, 0:HD],
                                  sbr[:, hd, LS:LS + QC].unsqueeze(1).to_broadcast([1, 2, QC]),
                                  start=False, stop=False, skip_group_check=True)
                        pe.matmul(o[:, 0:NSAMP], v[0:NSAMP, 0, hd * HD:(hd + 1) * HD], wssv[:, hd, :],
                                  start=False, stop=True, skip_group_check=True)
                        for t in range(1, 3):
                            t0 = TILES[t][0]
                            mm = pe.matmul(o[:, t0:t0 + P], v[:, t, hd * HD:(hd + 1) * HD], wst[:, hd, :],
                                           start=False, stop=True, skip_group_check=True)
                    mm.then_inc(sgu_mm, 1)
                for q in range(MT):
                    pe.wait_ge(y_ready, 4 * (l + 1))
                    if q >= 2:
                        pe.wait_ge(ya_ready, 4 * l + q - 1)
                    for z in range(2):
                        b = [1, 2][z] if q % 2 == 0 else [3, 0][z]
                        mm = pe.matmul(bank(b), glu[:, q, z, :], ua[:, q, :], start=True, stop=True)
                    mm.then_inc(glu_mm, 1)
                pe.wait_ge(yb_ready, 4 * (l + 1))
                mean_sum(h, MT, MT, 4, 24 * l + 8)
                mean_sum(h, 0, MT, 5, 24 * l + 12)
                for m in range(KT):
                    if m >= 4:
                        pe.wait_ge(xadd, X_OUT[l] + m - 3)
                    for k in range(KT):
                        if m == 0:
                            pe.wait_ge(h_ready, 24 * l + 8 + k + 1)
                            pe.wait_ge(d_in[k // 2], 16 * (1 if l == 0 else (4 if k < 6 else 6)))
                        mm = pe.matmul(bank(m % 4), w_out[:, k, m * P:(m + 1) * P], h[:, k, :],
                                       start=(k == 0), stop=(k == KT - 1))
                    mm.then_inc(wo_mm, 1)
                mean_sum(sq2, 0, KT, 6, 24 * l + 16)
                if l == 0:
                    for hf in range(2):
                        for m in range(FT):
                            if m >= 4:
                                pe.wait_ge(hid_ready, FT * hf + m - 3)
                            elif hf:
                                pe.wait_ge(xadd, X_DENSE[0] + 2 * m + 2)
                            r = rows(m)
                            for z, (w, used, sems) in enumerate([(gate, gate_used, g_in), (up, up_used, u_in)]):
                                for k in range(KT):
                                    if m == 0:
                                        pe.wait_ge(h_ready, 16 + k + 1)
                                        pe.wait_ge(sems[k // 2], 16 * (hf + 1 + (z == 0)))
                                    mm = pe.matmul(ps[0:r, 2 * (m % 4) + z, 0:T], w[:, k, m * P:m * P + r],
                                                   h[:, k, :], start=(k == 0), stop=(k == KT - 1))
                                    if m == FT - 1 and k % 2 == 1 and not (z == 1 and k == KT - 1):
                                        mm.then_inc(used, 1)
                            mm.then_inc(gu_mm, 1)
                        pe.wait_ge(hid_ready, FT * (hf + 1))
                        for m in range(KT):
                            for j, (a, b) in enumerate(DPIECE):
                                for kk in range(a, b):
                                    if m == 0 and kk == a:
                                        pe.wait_ge(d_in[j], 16 * (hf + 2) if j < 3 else 16 * (2 * hf + 3))
                                    r = rows(kk)
                                    mm = pe.matmul(bank(m), down[0:r, kk, m * P:(m + 1) * P], hid[0:r, kk, :],
                                                   start=(kk == 0), stop=(kk == FT - 1))
                                if m == KT - 1 and j < PIECES - 1:
                                    mm.then_inc(down_used, 1)
                            mm.then_inc(dn_mm, 1)
            pe.wait_ge(h_ready, 48)
            for t, (t0, n) in enumerate(TILES):
                for k in range(KT):
                    mm = pe.matmul(ps[0:n, 0, 8 * t:8 * t + 8], h[:, k, t0:t0 + n], rw[:, k, :],
                                   start=(k == 0), stop=(k == KT - 1))
            mm.then_inc(lg_mm, 1)
            for n in range(6):
                t0, w = TILES[n // 2]
                for k in range(4):
                    mm = pe.transpose(ps[0:w, n + 1, k * P:(k + 1) * P], h[:, 4 * (n % 2) + k, t0:t0 + w], ident)
                mm.then_inc(htok_mm, 1)
            pe.wait_ge(mask_ready, 3)
            for t, (t0, n) in enumerate(TILES):
                for u in range(t + 1):
                    w = TILES[u][1]
                    lhs = strict[0:w, 0:n] if u == t else ones[0:w, 0:n]
                    pe.matmul(ps[0:n, 7, 8 * t:8 * t + 8], lhs, mask[0:w, u, :], start=(u == 0), stop=(u == t))
            for u, (_, w) in enumerate(TILES):
                mm = pe.matmul(ps[:, 7, 24:32], ones[0:w, :], mask[0:w, u, :], start=(u == 0), stop=(u == 2))
            mm.then_inc(pos_mm, 1)
            pe.wait_ge(htok_ready, 6)
            pe.wait_ge(ni_ready, 1)
            turns = pe.value_load(ni_sb[0:1, 0:1], min_val=NE, max_val=MAXPASS * NE)
            with pe.Fori(0, turns) as i:
                pe.wait_ge(oh_ready, i + 1)
                pe.wait_ge(xadd, 8 * i + X_MOE)
                for t in (1, 2, 0):
                    t0, n = TILES[t]
                    mm = pe.transpose(bank(0, n, t0), goh[0:n, t, :], ident[0:n, 0:n])
                mm.then_inc(gtr_mm, 1)
                for k in range(KT):
                    for t, (_, n) in enumerate(TILES):
                        mm = pe.matmul(bank(6 + k // 4, P, (k % 4) * P), h_tok[0:n, t, k * P:(k + 1) * P],
                                       oh[0:n, t, :], start=(t == 0), stop=(t == 2))
                    if k % 4 == 3:
                        mm.then_inc(gather_mm, 1)
                pe.wait_ge(sgt_ready, i + 1)
                for k in range(KT):
                    if k % 4 == 0:
                        pe.wait_ge(hg_ready, 2 * i + (k // 4 + 1))
                    if k % 2 == 0:
                        pe.wait_ge(g_in[k // 2], 16 * i + 80)
                        pe.wait_ge(u_in[k // 2], 16 * i + 48)
                    st, sp_ = (k == 0), (k == KT - 1)
                    if k < KT - 1:
                        for z, (w, used) in enumerate([(gate, gate_used), (up, up_used)]):
                            for c, (a, b) in enumerate(FCH):
                                mm = pe.matmul(ps[:, 3 * z + c, 0:b - a], hg[:, k, :], w[:, k, a:b],
                                               start=st, stop=sp_)
                            if k % 2 == 1:
                                mm.then_inc(used, 1)
                    else:
                        for c, (a, b) in enumerate(FCH):
                            mg = pe.matmul(ps[:, c, 0:b - a], hg[:, k, :], gate[:, k, a:b], start=st, stop=sp_)
                            mm = pe.matmul(ps[:, 3 + c, 0:b - a], hg[:, k, :], up[:, k, a:b], start=st, stop=sp_)
                            if c == 2:
                                mg.then_inc(gate_used, 1)
                            mm.then_inc(egu_mm, 1)
                for c in range(3):
                    pe.wait_ge(he_ready, 3 * i + (c + 1))
                    for kk in range(4 * c, min(4 * c + 4, FT)):
                        r = rows(kk)
                        mm = pe.transpose(ps[0:r, c, (kk % 4) * P:(kk % 4 + 1) * P], he[:, kk * P:kk * P + r],
                                          ident)
                    mm.then_inc(etr_mm, 1)
                for j, (a, b) in enumerate(DPIECE):
                    pe.wait_ge(d_in[j], 16 * i + 80 if j < 3 else 32 * i + 128)
                    for kk in range(a, b):
                        if kk % 4 == 0:
                            pe.wait_ge(het_ready, 4 * i + (kk // 4 + 1))
                        if kk == FT - 1:
                            pe.wait_ge(het_ready, 4 * i + 4)
                        r = rows(kk)
                        for z in range(2):
                            mm = pe.matmul(ps[:, 6 + z, :], het[0:r, kk, :], down[0:r, kk, 512 * z:512 * z + 512],
                                           start=(kk == 0), stop=(kk == FT - 1))
                    mm.then_inc(down_used if j < PIECES - 1 else ed_mm, 1)
                for k in range(KT):
                    if k % 4 == 0:
                        pe.wait_ge(ye_ready, 2 * i + (k // 4 + 1))
                    if k >= 6:
                        pe.wait_ge(xadd, 8 * i + (X_MOE + k - 5))
                    pe.matmul(bank((3 + k) % 6), ye[:, k * P:(k + 1) * P], sgt,
                              start=True, stop=True).then_inc(sc_mm, 1)
            mean_sum(h, 0, KT, 7, 48)

        @block.vector
        def _(dve):
            n_chain = [0]

            def link(ins):
                n_chain[0] += 1
                ins.then_inc(dve_chain, 1)
                dve.wait_ge(dve_chain, n_chain[0])

            def tt(o, a, b, op):
                return dve.tensor_tensor(o, a, b, op)

            def normalise(n, slot, pairs):
                dve.wait_ge(sd_ready, n)
                r = rs[:, slot * T:(slot + 1) * T]
                link(dve.reciprocal(r, r))
                for dst, src, gain in pairs:
                    dve.scalar_tensor_tensor(dst, src, gain, r, ALU.mult, ALU.mult).then_inc(h_ready, 1)

            def add_to_x(k, b):
                tt(x[:, k, :], x[:, k, :], bank(b), ALU.add).then_inc(xadd, 1)

            link(dve.memset(eps[:, :], EPS))
            dve.wait_ge(const_in, 48)
            for l in range(DEPTH):
                dve.tensor_scalar(hb2[:, 4 * l:4 * l + 4], col(l, "glu_b2", 0, 4), 0.5, None, ALU.mult)
            for l in range(DEPTH):
                normalise(4 * l + 1, 0, [(h[:, k, :], x[:, k, :], col(l, "norm_mix", k)) for k in range(KT)])
                are, aim = col(l, "a_re", 0, 16), col(l, "a_im", 0, 16)
                dve.wait_ge(dt_ready, l + 1)
                tt(sv(1), are, sv(0), ALU.mult)
                tt(sv(2), aim, sv(0), ALU.mult).then_inc(th_ready, 1)
                dve.wait_ge(th_ready, l + 1)
                link(dve.tensor_scalar(sv(9), sv(2), 1.0 / TWO_PI, ROUND, ALU.mult, ALU.add))
                link(dve.tensor_scalar(sv(9), sv(9), ROUND, None, ALU.subtract))
                link(dve.scalar_tensor_tensor(sv(5), sv(9), -C1, sv(2), ALU.mult, ALU.add))
                link(dve.scalar_tensor_tensor(sv(5), sv(9), -C2, sv(5), ALU.mult, ALU.add))
                link(dve.tensor_scalar(sv(5), sv(5), PI_SAFE, -PI_SAFE, ALU.min, ALU.max))
                link(dve.tensor_scalar(sv(6), sv(5), -1.0, None, ALU.mult))
                link(tt(sv(6), sv(5), sv(6), ALU.min))
                dve.tensor_scalar(sv(6), sv(6), TWO_PI / 4, None, ALU.add).then_inc(ang_ready, 1)
                dve.wait_ge(mag_ready, l + 1)
                dve.wait_ge(trig_ready, l + 1)
                dve.wait_ge(ang_ready, l + 1)
                sn, cs = sv(7), sv(8)
                tt(sv(10), sv(3), cs, ALU.mult)
                tt(sv(11), sv(3), sn, ALU.mult)
                tt(sv(17), cs, cs, ALU.mult)
                tt(sv(18), sn, sn, ALU.mult)
                link(tt(sv(19), cs, sn, ALU.mult))
                tt(sv(17), sv(17), sv(18), ALU.subtract)
                link(tt(sv(19), sv(19), sv(19), ALU.add))
                tt(sv(20), sv(17), sv(17), ALU.mult)
                tt(sv(21), sv(19), sv(19), ALU.mult)
                link(tt(sv(22), sv(17), sv(19), ALU.mult))
                tt(sv(12), sv(20), sv(21), ALU.subtract)
                link(tt(sv(13), sv(22), sv(22), ALU.add))
                tt(a4[:, 0:NP], sv(4), sv(12), ALU.mult)
                tt(a4[:, NP:2 * NP], sv(4), sv(13), ALU.mult).then_inc(a_ready, 1)
                dve.wait_ge(a_ready, l + 1)
                link(dve.tensor_copy(mag_tab, bc(sv(4), NCP)))
                dve.memset(mag_tab[:, :, 0:1], 0.0)
                dve.tensor_scalar(sv(23), sv(10), -1.0, None, ALU.add)
                tt(sv(24), are, are, ALU.mult)
                link(tt(sv(25), aim, aim, ALU.mult))
                link(tt(sv(24), sv(24), sv(25), ALU.add))
                dve.reciprocal(sv(24), sv(24))
                tt(sv(26), sv(23), are, ALU.mult)
                tt(sv(27), sv(11), aim, ALU.mult)
                tt(sv(28), sv(11), are, ALU.mult)
                link(tt(sv(29), sv(23), aim, ALU.mult))
                tt(sv(26), sv(26), sv(27), ALU.add)
                link(tt(sv(28), sv(28), sv(29), ALU.subtract))
                tt(sv(26), sv(26), sv(24), ALU.mult)
                link(tt(sv(28), sv(28), sv(24), ALU.mult))
                dve.wait_ge(prep_in, 48 * (l + 1))
                for s in range(CH):
                    fr, fi = (bc(sv(26), 32), bc(sv(28), 32)) if s == 0 else (bc(sv(10), 32), bc(sv(11), 32))
                    br, bi = BPX[:, 0, max(s - 1, 0), :, :], BPX[:, 1, max(s - 1, 0), :, :]
                    o_r, o_i = BPX[:, 0, s, :, :], BPX[:, 1, s, :, :]
                    tt(bt1, fi, bi, ALU.mult)
                    link(tt(bt2, fi, br, ALU.mult))
                    tt(o_r, fr, br, ALU.mult)
                    link(tt(o_i, fr, bi, ALU.mult))
                    tt(o_r, o_r, bt1, ALU.subtract)
                    last = tt(o_i, o_i, bt2, ALU.add)
                    if s < CH - 1:
                        link(last)
                    else:
                        last.then_inc(bp_ready, 1)
                link(dve.memset(var[:, :], 1.0))
                dve.wait_ge(mix_in, 112 * (l + 1))
                for t, (_, n) in enumerate(TILES):
                    vt = v[0:n, t, :].rearrange("p (h d) -> p h d", h=NH)
                    m_, v_ = mu[0:n, 8 * t:8 * t + 8], var[0:n, 8 * t:8 * t + 8]
                    dve.wait_ge(v_ready, 3 * l + t + 1)
                    link(dve.tensor_reduce(m_, vt, AX.X, ALU.add))
                    link(dve.tensor_scalar(m_, m_, 1.0 / HD, None, ALU.mult))
                    link(tt(vt, vt, bc(m_, HD), ALU.subtract))
                    sqv = lt[0:n, :].rearrange("p (h d) -> p h d", h=NH)
                    link(tt(sqv, vt, vt, ALU.mult))
                    link(dve.tensor_reduce(v_, sqv, AX.X, ALU.add))
                link(dve.tensor_scalar(var[:, :], var[:, :], 1.0 / HD, EPS, ALU.mult, ALU.add))
                yi, yt = nwt[:, 0:24], nwt[:, 24:48]
                link(dve.tensor_scalar(yi.bitcast(I32), var[:, :].bitcast(I32), 1, None, ALU.logical_shift_right))
                link(dve.tensor_scalar(yi.bitcast(I32), yi.bitcast(I32), -1.0, float(0x5F3759DF), ALU.mult, ALU.add))
                for _ in range(4):
                    link(tt(yt, yi, yi, ALU.mult))
                    link(tt(yt, yt, var[:, :], ALU.mult))
                    link(dve.tensor_scalar(yt, yt, -0.5, 1.5, ALU.mult, ALU.add))
                    link(tt(yi, yi, yt, ALU.mult))
                for t, (_, n) in enumerate(TILES):
                    vt = v[0:n, t, :].rearrange("p (h d) -> p h d", h=NH)
                    link(tt(vt, vt, bc(nwt[0:n, 8 * t:8 * t + 8], HD), ALU.mult))
                    link(tt(v[0:n, t, :], v[0:n, t, :], lng[0:n, :], ALU.mult))
                    tt(v[0:n, t, :], v[0:n, t, :], lnb[0:n, :], ALU.add).then_inc(vn_ready, 1)
                dve.wait_ge(rot_ready, l + 1)
                dve.wait_ge(set_ready, 2 * (l + 1))
                if l:
                    dve.wait_ge(fin_out, 32 * l)
                f_r = fin[:, 0:128].rearrange("p (n c) -> p n c", n=NP)
                f_i = fin[:, 128:256].rearrange("p (n c) -> p n c", n=NP)
                h0r, h0i = S[:, 0, :, 0:NCS], S[:, 1, :, 0:NCS]
                a4r, a4i = bc(a4[:, 0:NP], NCS), bc(a4[:, NP:2 * NP], NCS)
                t8a = lt[:, 0:128].rearrange("p (n c) -> p n c", n=NP)
                t8b = lt[:, 128:256].rearrange("p (n c) -> p n c", n=NP)
                tt(f_r, a4r, h0r, ALU.mult)
                tt(f_i, a4r, h0i, ALU.mult)
                tt(t8a, a4i, h0i, ALU.mult)
                link(tt(t8b, a4i, h0r, ALU.mult))
                tt(f_r, f_r, t8a, ALU.subtract)
                link(tt(f_i, f_i, t8b, ALU.add))

                def v4(ap):
                    return ap.rearrange("p (n c) -> p n c", n=4)

                for q in range(MT):
                    if q:
                        dve.wait_ge(st_ready, 4 * l + q)
                    dve.wait_ge(s_mm, 4 * l + q + 1)
                    quad = ps[:, 4:8, :] if q % 2 == 0 else ps[:, 0:4, :]
                    sr, si = quad[:, :, NCS:NCH], quad[:, :, NCH + NCS:2 * NCH]
                    n4 = slice(4 * q, 4 * q + 4)
                    cr, ci = rot[:, 0, n4, :], rot[:, 1, n4, :]
                    tt(f_r[:, n4, :], f_r[:, n4, :], quad[:, :, 0:NCS], ALU.add)
                    tt(f_i[:, n4, :], f_i[:, n4, :], quad[:, :, NCH:NCH + NCS], ALU.add)
                    tt(v4(wr), sr, cr, ALU.mult)
                    link(tt(v4(tmp), si, ci, ALU.mult))
                    link(tt(wr, wr, tmp, ALU.add))
                    tt(v4(wi), si, cr, ALU.mult)
                    tt(v4(tmp), sr, ci, ALU.mult).then_inc(s_used, 1)
                    dve.wait_ge(s_used, 4 * l + q + 1)
                    link(tt(wi, wi, tmp, ALU.subtract))
                    mg = mag_tab[:, n4, :].rearrange("p n c -> p (n c)")
                    dve.tensor_tensor_scan(wr, mg, wr, 0.0, ALU.mult, ALU.add)
                    link(dve.tensor_tensor_scan(wi, mg, wi, 0.0, ALU.mult, ALU.add))
                    or_, oi = S[:, 0, n4, NCS + 1:NCH + 1], S[:, 1, n4, NCS + 1:NCH + 1]
                    tt(or_, v4(wr), cr, ALU.mult)
                    link(tt(v4(tmp), v4(wi), ci, ALU.mult))
                    link(tt(or_, or_, v4(tmp), ALU.subtract))
                    tt(oi, v4(wi), cr, ALU.mult)
                    link(tt(v4(tmp), v4(wr), ci, ALU.mult))
                    tt(oi, oi, v4(tmp), ALU.add).then_inc(st_ready, 1)
                dve.wait_ge(st_ready, 4 * (l + 1))
                dve.tensor_copy(finp[:, 0:NP], S[:, 0, :, NCH])
                dve.tensor_copy(finp[:, NP:2 * NP], S[:, 1, :, NCH]).then_inc(fin_ready, 1)
                dve.wait_ge(k_mm, l + 1)
                for pp in range(4):
                    a, b = 32 * pp, 32 * pp + 32
                    last = dve.tensor_copy(Kt[a:b, :, :, a:b],
                                           ps[a:b, 0, :].rearrange("p (q s f) -> p q s f", q=MT, s=CH))
                link(last)
                for q in range(MT):
                    last = dve.scalar_tensor_tensor(Kt[:, q, 0, :], ident, col(l, "ssm_d", q), Kt[:, q, 0, :],
                                                    ALU.mult, ALU.add)
                last.then_inc(k_ready, 1)
                for ft in range(MT):
                    dve.wait_ge(sgu_mm, 4 * l + ft + 1)
                    dve.wait_ge(ub_ready, 4 * l + ft + 1)
                    tt(ub[:, ft, :], ub[:, ft, :], bank(4 + ft), ALU.mult).then_inc(yb_ready, 1)
                for q in range(MT):
                    dve.wait_ge(th2_ready, 4 * l + q + 1)
                    s_ = sg[:, (q % 2) * T:(q % 2 + 1) * T]
                    link(dve.tensor_scalar(s_, s_, 0.5, 0.5, ALU.mult, ALU.add))
                    dve.scalar_tensor_tensor(ua[:, q, :], bank(1 if q % 2 == 0 else 3), col(l, "glu_b1", q), s_,
                                             ALU.add, ALU.mult).then_inc(ya_ready, 1)
                dve.wait_ge(ya_ready, 4 * (l + 1))
                dve.wait_ge(yb_ready, 4 * (l + 1))
                dve.wait_ge(sd_ready, 4 * l + 3)
                link(dve.reciprocal(rs[:, :], rs[:, :]))
                for k in range(KT):
                    src, gain = (ua, "out_norm_a") if k < MT else (ub, "out_norm_b")
                    slot = 0 if k < MT else 1
                    dve.scalar_tensor_tensor(h[:, k, :], src[:, k % MT, :], col(l, gain, k % MT),
                                             rs[:, slot * T:(slot + 1) * T],
                                             ALU.mult, ALU.mult).then_inc(h_ready, 1)
                for m in range(KT):
                    dve.wait_ge(wo_mm, 8 * l + m + 1)
                    add_to_x(m, m % 4)
                dve.wait_ge(xadd, X_OUT[l] + 8)
                normalise(4 * l + 4, 0, [(h[:, k, :], x[:, k, :], col(l, "norm_ffn", k)) for k in range(KT)])
                if l == 0:
                    for hf in range(2):
                        for m in range(FT):
                            n = FT * hf + m
                            r = rows(m)
                            if m == 0 and hf:
                                dve.wait_ge(dn_mm, 8)
                            dve.wait_ge(silu_ready, n + 1)
                            tt(hid[0:r, m, :], sg[0:r, (n % 2) * T:(n % 2 + 1) * T],
                               ps[0:r, 2 * (m % 4) + 1, 0:T], ALU.mult).then_inc(hid_ready, 1)
                        for m in range(KT):
                            dve.wait_ge(dn_mm, 8 * hf + m + 1)
                            if hf:
                                dve.wait_ge(xadd, X_DENSE[0] + m + 1)
                            add_to_x(m, m)
                    dve.wait_ge(xadd, X_DENSE[1] + 8)
            for ap in (small[:, :], postab[:, :], gatetab[:, :]):
                last = dve.memset(ap, 0.0)
            link(last)
            dve.wait_ge(lg_mm, 1)
            for t, (_, n) in enumerate(TILES):
                last = tt(lg[0:n, t, :], ps[0:n, 0, 8 * t:8 * t + 8], rb[0:n, :], ALU.add)
            link(last)
            for t, (_, n) in enumerate(TILES):
                last = dve.max(m8[0:n, t, :], lg[0:n, t, :])
            link(last)
            for t, (_, n) in enumerate(TILES):
                dve.max_index(ixv[0:n, t, :], m8[0:n, t, :], lg[0:n, t, :])
            tt(cn, m8[:, :, 1], m8[:, :, 0], ALU.subtract).then_inc(d_ready, 1)
            dve.wait_ge(e_ready, 1)
            dve.wait_ge(d_ready, 1)
            link(dve.tensor_scalar(w0, e1, 1.0, None, ALU.add))
            link(dve.reciprocal(w0, w0))
            link(tt(w1, w0, e1, ALU.mult))
            for t, (_, n) in enumerate(TILES):
                link(dve.tensor_copy(ixf[0:n, t, 0:2], ixv[0:n, t, 0:2]))
                i0, i1 = ixf[0:n, t, 0:1], ixf[0:n, t, 1:2]
                i8 = iota[0:n, 0:NE]
                dve.tensor_scalar(mask[0:n, t, :], i8, i0, None, ALU.is_equal)
                dve.tensor_scalar(r8[0:n, t, :], i8, i1, None, ALU.is_equal)
                link(dve.tensor_scalar(gts[0:n, t, :], i8, i0, w0[0:n, t:t + 1], ALU.is_equal, ALU.mult))
                link(dve.scalar_tensor_tensor(gts[0:n, t, :], r8[0:n, t, :], w1[0:n, t:t + 1], gts[0:n, t, :],
                                              ALU.mult, ALU.add))
                tt(mask[0:n, t, :], mask[0:n, t, :], r8[0:n, t, :], ALU.add).then_inc(mask_ready, 1)
            dve.wait_ge(mask_ready, 3)
            dve.wait_ge(pos_mm, 1)
            link(dve.tensor_reduce(cn[:, 0:1], ps[:, 7, 24:32], AX.X, ALU.max))
            dve.tensor_scalar(cn[:, 1:2], cn[:, 0:1], 128.0, 8.0, ALU.is_gt, ALU.mult)
            link(dve.tensor_scalar(cn[:, 2:3], cn[:, 0:1], 256.0, 8.0, ALU.is_gt, ALU.mult))
            link(tt(cn[:, 1:2], cn[:, 1:2], cn[:, 2:3], ALU.add))
            dve.tensor_scalar(ni_sb[:, :], cn[:, 1:2], 8.0, None, ALU.add).then_inc(ni_ready, 1)
            for t, (_, n) in enumerate(TILES):
                link(dve.tensor_scalar(r8[0:n, t, :], mask[0:n, t, :], 1000.0, -1000.0, ALU.mult, ALU.add))
                link(tt(r8[0:n, t, :], r8[0:n, t, :], ps[0:n, 7, 8 * t:8 * t + 8], ALU.add))
                for r in range(MAXPASS):
                    dve.tensor_scalar(pos[0:n, t, NE * r:NE * r + NE], r8[0:n, t, :], -128.0 * r, None, ALU.add)
                    last = dve.tensor_copy(gat[0:n, t, NE * r:NE * r + NE], gts[0:n, t, :])
            link(last)

            def one_hots(i):
                for t, (_, n) in enumerate(TILES):
                    dve.tensor_scalar(oh[0:n, t, :], iota[0:n, :], pos[0:n, t, bass.ds(i, 1)], None, ALU.is_equal)
                    last = dve.tensor_scalar(goh[0:n, t, :], iota[0:n, :], pos[0:n, t, bass.ds(i, 1)],
                                             gat[0:n, t, bass.ds(i, 1)], ALU.is_equal, ALU.mult)
                last.then_inc(oh_ready, 1)

            one_hots(0)
            dve.wait_ge(ni_ready, 1)
            turns = dve.value_load(ni_sb[0:1, 0:1], min_val=NE, max_val=MAXPASS * NE)
            with dve.Fori(0, turns) as i:
                dve.wait_ge(gtr_mm, i + 1)
                dve.tensor_copy(sgt, bank(0)).then_inc(sgt_ready, 1)
                for c, (a, b) in enumerate(FCH):
                    dve.wait_ge(esilu_ready, 3 * i + (c + 1))
                    tt(he[:, a:b], sge[:, a:b], ps[:, 3 + c, 0:b - a], ALU.mult).then_inc(he_ready, 1)
                one_hots(i + 1)
                for k in range(KT):
                    dve.wait_ge(sc_mm, 8 * i + (k + 1))
                    dve.wait_ge(xadd, 8 * i + (X_MOE - 8 + k + 1))
                    add_to_x(k, (3 + k) % 6)
            dve.wait_ge(xadd, 8 * turns + X_MOE)
            normalise(9, 0, [(h[:, k, :], x[:, k, :], cols[:, DEPTH * NCOL + k:DEPTH * NCOL + k + 1])
                             for k in range(KT)])



def _by_feature(a, n):
    return a.reshape(n, P).T


def _pair_blocks(a):
    out = np.zeros((P, NP, 2 * GH), np.float32)
    for g in range(2):
        out[g * NST:(g + 1) * NST, :, g * GH:(g + 1) * GH] = a[g::2].transpose(1, 0, 2)
    return out


def _by_state(a):
    return np.moveaxis(a.reshape((NP, 2 * NST) + a.shape[2:]), 0, 1)


def kernel(**inputs):
    import concourse.bacc as bacc
    from concourse.bass_utils import run_bass_kernel_spmd as run

    w = {k: np.asarray(a) for k, a in inputs.items()}
    f = np.float32
    tokens = np.concatenate([w["x_sample"].reshape(NSAMP, DM), w["x_prompt"].reshape(NPROMPT, DM)])
    d = {}
    d["x"] = tokens.T.reshape(KT, P, T).transpose(1, 0, 2)
    r = np.arange(P)
    d["consts"] = np.concatenate([np.eye(P, dtype=f), (r[:, None] <= r[None, :]).astype(f),
                                  (r[:, None] < r[None, :]).astype(f),
                                  np.broadcast_to(r[None, :].astype(f), (P, P)), np.ones((P, P), f)], 1)
    cols = []
    glu = np.zeros((DEPTH, P, MT, 2, P), f)
    for l in range(DEPTH):
        b = w["glu_b"][l]
        cols += [_by_feature(w["norm_mix"][l], KT), _by_feature(w["out_norm_a"][l], MT),
                 _by_feature(w["out_norm_b"][l], MT), _by_feature(w["norm_ffn"][l], KT),
                 _by_feature(b[:, :GH].reshape(-1), MT), _by_feature(b[:, GH:].reshape(-1), MT),
                 _by_feature(w["ssm_d"][l].reshape(-1), MT),
                 _by_state(w["ssm_a_re"][l]), _by_state(w["ssm_a_im"][l]),
                 _by_state(np.repeat(w["ssm_log_dt"][l][:, None], NST, 1))]
        gw = w["glu_w"][l].reshape(MT, 8, GH, 2, GH)
        for g in range(8):
            glu[l, g * GH:(g + 1) * GH, :, :, g * GH:(g + 1) * GH] = gw[:, g].transpose(1, 0, 2, 3)
    cols.append(_by_feature(w["norm_final"], KT))
    d["cols"] = np.concatenate(cols, 1)
    d["misc"] = np.concatenate([w["router_w"][0].reshape(KT, P, NE).transpose(1, 0, 2).reshape(P, KT * NE),
                                np.broadcast_to(w["router_b"][0][None, :], (P, NE))], 1)
    d["w_in"], d["w_out"] = w["w_in"], w["w_out"]
    d["b"] = np.stack([np.stack([_pair_blocks(w["ssm_b_re"][l]), _pair_blocks(w["ssm_b_im"][l])], 1)
                       for l in range(DEPTH)])
    d["c"] = np.stack([np.stack([_pair_blocks(w["ssm_c_re"][l].transpose(0, 2, 1)),
                                 _pair_blocks(w["ssm_c_im"][l].transpose(0, 2, 1))], 1)
                       for l in range(DEPTH)])
    d["glu"] = glu
    d["ln"] = np.broadcast_to(np.concatenate([w["sgu_ln_g"].reshape(DEPTH, MIX), w["sgu_ln_b"].reshape(DEPTH, MIX)],
                                             1)[:, None, :], (DEPTH, P, 2 * MIX))
    wt = w["sgu_w"].transpose(0, 3, 1, 2)
    d["wst"] = wt
    wss = np.zeros((DEPTH, BS, LS, NH, BS, LS), f)
    for b in range(BS):
        wss[:, b, :, :, b, :] = wt[:, :LS, :, :LS]
    d["wss"] = wss.reshape(DEPTH, NSAMP, NH * NSAMP)
    d["sbias"] = np.concatenate([w["sgu_b"][:, :, :LS], w["sgu_b"]], 2).reshape(DEPTH, NH * (LS + QC))
    h0 = []
    for l in range(DEPTH):
        h0.append(np.stack([_by_state(w[n][l].transpose(1, 2, 0)) for n in ("state_ssm_re", "state_ssm_im")], 1))
    d["h0"] = np.stack(h0)
    for n in ("ffn_w_gate", "ffn_w_up", "ffn_w_down"):
        d[n] = w[n]
    for n in ("moe_w_gate", "moe_w_up", "moe_w_down"):
        d[n] = w[n][0]

    nc = bacc.Bacc("TRN2", target_bir_lowering=False, num_devices=1)
    arrays, args = {}, []
    for name, a in d.items():
        a = np.ascontiguousarray(a)
        arrays[f"in_{name}"] = a
        args.append(nc.dram_tensor(f"in_{name}", list(a.shape), F32, kind="ExternalInput").ap())
    outs = {"y": (P, KT, T), "sp": (DEPTH, P, 2 * NP), "ss": (DEPTH, P, 2 * NP * NCS), "vn": (DEPTH, NSAMP, MIX)}
    for name, shape in outs.items():
        args.append(nc.dram_tensor(f"out_{name}", list(shape), F32, kind="ExternalOutput").ap())
    build(nc, *args)
    res = run(nc, [arrays], core_ids=[0]).results[0]

    y = np.asarray(res["out_y"]).transpose(2, 1, 0).reshape(T, DM)
    sp = np.asarray(res["out_sp"]).reshape(DEPTH, 2, NST, 2, NP)
    ss = np.asarray(res["out_ss"]).reshape(DEPTH, 2, NST, 2, NP, BS)
    sp = sp.transpose(3, 0, 4, 1, 2).reshape(2, DEPTH, 1, NG, NST)
    ss = ss.transpose(3, 0, 5, 4, 1, 2).reshape(2, DEPTH, BS, NG, NST)
    vn = np.asarray(res["out_vn"]).reshape(DEPTH, BS, LS, NH, HD)
    return (np.ascontiguousarray(y[NSAMP:]).reshape(1, NPROMPT, DM), np.ascontiguousarray(y[:NSAMP]).reshape(BS, LS, DM),
            np.ascontiguousarray(sp[0]), np.ascontiguousarray(sp[1]),
            np.ascontiguousarray(ss[0]), np.ascontiguousarray(ss[1]), np.ascontiguousarray(vn))
```

```python
from contextlib import ExitStack

import numpy as np

import concourse.bass as bass
from concourse import mybir

F32 = mybir.dt.float32
F32R = mybir.dt.float32r
I32 = mybir.dt.int32
U32 = mybir.dt.uint32
ALU = mybir.AluOpType
ACT = mybir.ActivationFunctionType
AX = mybir.AxisListType

P = 128
DEPTH = 2
DM = 1024
KT = DM // P
BS, LS = 8, 4
NSAMP = BS * LS
NPROMPT = 256
T = NSAMP + NPROMPT
CH = 4
NCS = NSAMP // CH
NCP = NPROMPT // CH
NCH = NCS + NCP
TILES = [(0, NSAMP), (NSAMP, P), (NSAMP + P, P)]
MIX = DM // 2
MT = MIX // P
IN_W = 3 * MIX
NG, GH, NST = 32, 16, 64
NP = NG // 2
NH, HD = 8, 64
QC = 128
FF = 1376
FT = 11
NE = 8
EPS = 1e-6
PIECES = 4
FCH = [(0, 512), (512, 1024), (1024, FF)]
MAXPASS = 3
TAB = MAXPASS * NE + 1
TWO_PI = 6.283185307179586
C1 = 6.28125
C2 = TWO_PI - C1
ROUND = 12582912.0
PI_SAFE = 3.1415925

COLS = {}
_at = 0
for _name, _n in [("norm_mix", 8), ("out_norm_a", 4), ("out_norm_b", 4), ("norm_ffn", 8),
                  ("glu_b1", 4), ("glu_b2", 4), ("ssm_d", 4), ("a_re", 16), ("a_im", 16),
                  ("log_dt", 16)]:
    COLS[_name] = (_at, _n)
    _at += _n
NCOL = _at

X_OUT = [0, 24]
X_DENSE = [8, 16]
X_MOE = 32

NRAW, NSPLIT = 6, 9
HALF_CHUNKS = 33
DENSE = 2 * HALF_CHUNKS
EXP_CHUNKS = 2 * KT + FT
PAIR = 2 * EXP_CHUNKS
AHEAD = 6
SHIFT = 6
assert (DENSE + SHIFT) % NSPLIT == 0 and EXP_CHUNKS % NSPLIT == 0 and DENSE % NRAW == 0 and PAIR % NRAW == 0
POOL_SLOTS = (3, 7)
MPAIRS = 5


def by_pool(n):
    return (n + SHIFT) % NSPLIT in POOL_SLOTS


def lows_before(n, pool):
    return sum(by_pool(a) == pool for a in range(n))


PAIR_LOWS = {p: lows_before(DENSE + PAIR, p) - lows_before(DENSE, p) for p in (False, True)}


def bc(ap, n):
    return ap.unsqueeze(2).to_broadcast([ap.shape[0], ap.shape[1], n])


def rows(kk):
    return P if kk < FT - 1 else FF - P * (FT - 1)


def build(nc, x_d, consts_d, cols_d, misc_d, w_in_d, w_out_d, b_d, c_d, glu_d, ln_d, wst_d, wss_d,
          sbias_d, h0_d, ffn_g_d, ffn_u_d, ffn_d_d, moe_g_d, moe_u_d, moe_d_d,
          y_d, sp_d, ss_d, vn_d):
    ctx = ExitStack()
    with ctx:
        def sb(name, n, dt=F32):
            return ctx.enter_context(nc.sbuf_tensor(name, [P, n], dt))

        def sem(name):
            return ctx.enter_context(nc.semaphore(name))

        def over(*tensors):
            with ExitStack() as inner:
                return [inner.enter_context(nc.sbuf_tensor(name, [P, n], dt)) for name, n, dt in tensors]

        raw, split_g = over(("raw", NRAW * FF, F32), ("split_g", 2 * FF, F32R))
        G = sb("G", KT * IN_W)
        split_u, = over(("split_u", 8 * FF, F32R))
        U = sb("U", KT * FF)
        split_d, = over(("split_d", 8 * FF, F32R))
        D = sb("D", FT * DM)
        Md, = over(("Md", 2 * FT * T + KT * T, F32R))
        Me, = over(("Me", 9632, F32R))
        M = sb("M", 11584)
        xb = sb("xb", KT * T)
        hbr, = over(("hbr", KT * T, F32R))
        hb = sb("hb", KT * T)
        consts = sb("consts", 5 * P)
        cols = sb("cols", DEPTH * NCOL + 8)
        misc = sb("misc", 72)
        rs = sb("rs", 2 * T)
        sg = sb("sg", 2 * T)
        fin = sb("fin", 2 * NP * NCS)
        finp = sb("finp", 2 * NP)
        a4 = sb("a4", 2 * NP)
        hb2 = sb("hb2", DEPTH * 4)
        eps = sb("eps", 1)
        ni_sb = sb("ni_sb", 1, I32)

        x = xb[:, :].rearrange("p (k t) -> p k t", t=T)
        h = hb[:, :].rearrange("p (k t) -> p k t", t=T)
        ident = consts[:, 0:P]
        upper = consts[:, P:2 * P]
        strict = consts[:, 2 * P:3 * P]
        iota = consts[:, 3 * P:4 * P]
        ones = consts[:, 4 * P:5 * P]
        rw = misc[:, 0:64].rearrange("p (k e) -> p k e", e=NE)
        rb = misc[:, 64:72]
        sbr = M[0:1, 10272:11328].rearrange("p (h t) -> p h t", h=NH)
        wssv = M[0:NSAMP, 11328:11584].rearrange("p (h t) -> p h t", h=NH)

        def col(l, name, i=0, n=1):
            return cols[:, l * NCOL + COLS[name][0] + i:l * NCOL + COLS[name][0] + i + n]

        w_in = G[:, :].rearrange("p (k f) -> p k f", f=IN_W)
        w_out = D[:, 0:KT * DM].rearrange("p (k f) -> p k f", f=DM)
        BT = U[:, 0:4096].rearrange("p (r n s) -> p r n s", r=2, n=NP)
        CPX = U[:, 4096:9216].rearrange("p (r n s f) -> p r n s f", r=2, n=NP, s=CH + 1)
        mag_tab = U[:, 9216:10240].rearrange("p (n c) -> p n c", n=NP)
        wr = U[:, 10240:10496]
        wi = U[:, 10496:10752]
        tmp = U[:, 10752:11008]
        lt = U[:, 10240:10752]
        mu = U[:, 10752:10776]
        var = U[:, 10776:10800]
        nwt = U[:, 10800:10848]
        BPX = D[:, 0:4096].rearrange("p (r n s f) -> p r n s f", r=2, s=CH, n=NP)
        bt1 = D[:, 4096:4608].rearrange("p (n f) -> p n f", n=NP)
        bt2 = D[:, 4608:5120].rearrange("p (n f) -> p n f", n=NP)
        ust = D[:, 4096:5248].rearrange("p (q f c) -> p q f c", q=MT, f=4)
        sraw = [D[:, 2048 * r:2048 * (r + 1)].rearrange("p (n c) -> p n c", n=NP)[:, :, 32:32 + NCH]
                for r in range(2)]
        ct1 = D[:, 5248:5760].rearrange("p (n f) -> p n f", n=NP)
        ct2 = D[:, 5760:6272].rearrange("p (n f) -> p n f", n=NP)
        rt1 = D[:, 6272:6784]
        rt2 = D[:, 6784:7296]

        def sv(i, n=1):
            return D[:, 7296 + 16 * i:7296 + 16 * (i + n)]

        glu = D[:, 8192:9216].rearrange("p (q z f) -> p q z f", q=MT, z=2)
        lng = D[:, 9216:9728]
        lnb = D[:, 9728:10240]
        wst = D[:, 10240:11264].rearrange("p (h q) -> p h q", h=NH)
        Kt = M[:, 0:2048].rearrange("p (q s f) -> p q s f", q=MT, s=CH)
        rot = M[:, 2048:4096].rearrange("p (r n c) -> p r n c", r=2, n=NP)
        S = M[:, 4096:6432].rearrange("p (r n c) -> p r n c", r=2, n=NP)
        ua = M[:, 6432:7584].rearrange("p (q t) -> p q t", q=MT)
        ub = M[:, 7584:8736].rearrange("p (q t) -> p q t", q=MT)
        v = M[:, 8736:10272].rearrange("p (t f) -> p t f", t=3)
        sq2 = M[:, 0:KT * T].rearrange("p (k t) -> p k t", t=T)
        hid_h = Md[:, 0:FT * T].rearrange("p (m t) -> p m t", t=T)
        hid_l = Md[:, FT * T:2 * FT * T].rearrange("p (m t) -> p m t", t=T)
        h_h = Md[:, 2 * FT * T:].rearrange("p (k t) -> p k t", t=T)
        h_l = hbr[:, :].rearrange("p (k t) -> p k t", t=T)
        tok_h = Me[:, 0:3072].rearrange("p (t f) -> p t f", t=3)
        tok_l = Me[:, 3072:6144].rearrange("p (t f) -> p t f", t=3)
        het_h = Me[:, 6144:7552].rearrange("p (k s) -> p k s", k=FT)
        het_l = Me[:, 7552:8960].rearrange("p (k s) -> p k s", k=FT)
        ye_h, ye_l = Me[:, 6144:7168], Me[:, 7552:8576]
        oh = Me[:, 8960:9344].rearrange("p (t s) -> p t s", t=3)
        sgt = Me[:, 9344:9632]
        he = M[:, 9632:11008]
        goh = M[:, 11008:11392].rearrange("p (t s) -> p t s", t=3)
        hg_h = hbr[:, 0:1024].rearrange("p (k s) -> p k s", k=KT)
        hg_l = hbr[:, 1024:2048].rearrange("p (k s) -> p k s", k=KT)
        gslot = M[:, 11392:11393]

        def split_slot(n):
            s = (n + SHIFT) % NSPLIT
            where, k = {6: (split_g, 0), 7: (split_u, 0), 8: (split_u, 1), 0: (split_u, 2), 1: (split_u, 3),
                        2: (split_d, 0), 3: (split_d, 1), 4: (split_d, 2), 5: (split_d, 3)}[s]
            return where[:, 2 * k * FF:(2 * k + 1) * FF], where[:, (2 * k + 1) * FF:(2 * k + 2) * FF]

        def raw_slot(n):
            return raw[:, (n % NRAW) * FF:(n % NRAW + 1) * FF]

        def dense_chunk(n):
            c = n % HALF_CHUNKS
            if c < 4 * MPAIRS:
                return ("gate", "up")[c % 4 // 2], c // 4, c % 2, P, 4 * 2 * P
            if c < 4 * MPAIRS + 2:
                return ("gate", "up")[c % 2], MPAIRS, 0, P, KT * rows(FT - 1)
            kk = c - 4 * MPAIRS - 2
            return "down", kk, 0, rows(kk), DM

        def exp_chunk(c):
            if c < 2 * KT:
                return ("gate", "up")[c % 2], c // 2, P, FF
            return "down", c - 2 * KT, rows(c - 2 * KT), DM

        small = G[:, 11008:11168]
        lg = small[:, 0:24].rearrange("p (t e) -> p t e", t=3)
        m8 = small[:, 24:48].rearrange("p (t e) -> p t e", t=3)
        ixf = small[:, 48:72].rearrange("p (t e) -> p t e", t=3)
        mask = small[:, 72:96].rearrange("p (t e) -> p t e", t=3)
        gts = small[:, 96:120].rearrange("p (t e) -> p t e", t=3)
        e1 = small[:, 120:123]
        w0 = small[:, 123:126]
        w1 = small[:, 126:129]
        cn = small[:, 129:132]
        r8 = small[:, 136:160].rearrange("p (t e) -> p t e", t=3)
        ixv = G[:, 11168:11192].bitcast(U32).rearrange("p (t e) -> p t e", t=3)
        postab = G[:, 11192:11192 + 3 * TAB]
        gatetab = G[:, 11272:11272 + 3 * TAB]
        pos = postab[:, :].rearrange("p (t i) -> p t i", t=3)
        gat = gatetab[:, :].rearrange("p (t i) -> p t i", t=3)

        ps = ctx.enter_context(nc.psum_tensor("ps", [P, 8, 512], F32))

        def bank(b, n=T, at=0):
            return ps[:, b, at:at + n]

        x_in = sem("x_in")
        const_in = sem("const_in")
        prep_in = sem("prep_in")
        mix_in = sem("mix_in")
        w_in_in = [sem(f"w_in_in{j}") for j in range(PIECES)]
        w_out_in = [sem(f"w_out_in{j}") for j in range(PIECES)]
        raw_in = [sem(f"raw_in{j}") for j in range(NRAW)]
        out_done = sem("out_done")
        fin_out = sem("fin_out")
        vn_out = sem("vn_out")
        hi_done = sem("hi_done")
        lo_dve = sem("lo_dve")
        lo_pool = sem("lo_pool")
        chunk_used = sem("chunk_used")
        sq_ready = sem("sq_ready")
        ms_mm = sem("ms_mm")
        sd_ready = sem("sd_ready")
        h_ready = sem("h_ready")
        xadd = sem("xadd")
        dt_ready = sem("dt_ready")
        th_ready = sem("th_ready")
        mag_ready = sem("mag_ready")
        ang_ready = sem("ang_ready")
        trig_ready = sem("trig_ready")
        a_ready = sem("a_ready")
        bp_ready = sem("bp_ready")
        cp_ready = sem("cp_ready")
        rot_ready = sem("rot_ready")
        set_ready = sem("set_ready")
        bt_mm = sem("bt_mm")
        bt_ready = sem("bt_ready")
        ua_mm = sem("ua_mm")
        ua_ready = sem("ua_ready")
        v_mm = sem("v_mm")
        v_ready = sem("v_ready")
        vn_ready = sem("vn_ready")
        ub_mm = sem("ub_mm")
        ub_ready = sem("ub_ready")
        s_mm = sem("s_mm")
        ust_ready = sem("ust_ready")
        s_ready = sem("s_ready")
        st_ready = sem("st_ready")
        fin_ready = sem("fin_ready")
        k_mm = sem("k_mm")
        k_ready = sem("k_ready")
        y_mm = sem("y_mm")
        y_ready = sem("y_ready")
        sgu_mm = sem("sgu_mm")
        yb_ready = sem("yb_ready")
        wst_ready = sem("wst_ready")
        glu_mm = sem("glu_mm")
        th2_ready = sem("th2_ready")
        ya_ready = sem("ya_ready")
        wo_mm = sem("wo_mm")
        hh_ready = sem("hh_ready")
        hl_ready = sem("hl_ready")
        gu_mm = sem("gu_mm")
        silu_ready = sem("silu_ready")
        hid_ready = sem("hid_ready")
        hidh_ready = sem("hidh_ready")
        hidl_ready = sem("hidl_ready")
        dn_mm = sem("dn_mm")
        lg_mm = sem("lg_mm")
        htok_mm = sem("htok_mm")
        tokh_ready = sem("tokh_ready")
        tokl_ready = sem("tokl_ready")
        d_ready = sem("d_ready")
        e_ready = sem("e_ready")
        mask_ready = sem("mask_ready")
        pos_mm = sem("pos_mm")
        ni_ready = sem("ni_ready")
        zero_ready = sem("zero_ready")
        oh_ready = sem("oh_ready")
        goh_ready = sem("goh_ready")
        gtr_mm = sem("gtr_mm")
        sgt_ready = sem("sgt_ready")
        gather_mm = sem("gather_mm")
        hgh_ready = sem("hgh_ready")
        hgl_ready = sem("hgl_ready")
        egu_mm = sem("egu_mm")
        esilu_ready = sem("esilu_ready")
        he_ready = sem("he_ready")
        etr_mm = sem("etr_mm")
        heth_ready = sem("heth_ready")
        hetl_ready = sem("hetl_ready")
        ed_mm = sem("ed_mm")
        yeh_ready = sem("yeh_ready")
        yel_ready = sem("yel_ready")
        sc_mm = sem("sc_mm")
        dve_chain = sem("dve_chain")
        act_chain = sem("act_chain")
        pool_chain = sem("pool_chain")

        moe_g = moe_g_d.rearrange("e (k p) f -> e p k f", p=P)
        moe_u = moe_u_d.rearrange("e (k p) f -> e p k f", p=P)

        def wait_low(eng, n, base=None):
            pool = by_pool(n)
            k = lows_before(n, pool) + 1
            eng.wait_ge(lo_pool if pool else lo_dve, k if base is None else base * PAIR_LOWS[pool] + k)

        def dims(n):
            return dense_chunk(n)[3:] if n < DENSE else exp_chunk((n - DENSE) % EXP_CHUNKS)[2:]

        def per_expert(i, a, per, n):
            return i * (2 * per) + (per * a + n)

        def turn(n, i):
            return n if i is None else i * PAIR + n

        block = ctx.enter_context(nc.Block())

        @block.sync
        def _(sp):
            sp.dma_start(x, x_d).then_inc(x_in, 16)
            sp.dma_start(consts[:, :], consts_d).then_inc(const_in, 16)
            sp.dma_start(cols[:, :], cols_d).then_inc(const_in, 16)
            sp.dma_start(misc[:, :], misc_d).then_inc(const_in, 16)

            def load_in(l):
                src = w_in_d[l].rearrange("(k p) f -> p k f", p=P)
                for j, (k0, k1, f) in enumerate([(0, 4, 0), (4, KT, 0), (0, KT, 2 * MIX), (0, KT, MIX)]):
                    sp.dma_start(w_in[:, k0:k1, f:f + MIX], src[:, k0:k1, f:f + MIX]).then_inc(w_in_in[j], 16)

            def load_out(l):
                src = w_out_d[l].rearrange("(k p) f -> p k f", p=P)
                for j in range(PIECES):
                    sp.dma_start(w_out[:, 2 * j:2 * j + 2, :], src[:, 2 * j:2 * j + 2, :]).then_inc(w_out_in[j], 16)

            def raw_free(n, i=None):
                wait_low(sp, n - NRAW, i)

            load_in(0)
            for l in range(DEPTH):
                sp.wait_ge(bt_mm, 8 * (l + 1))
                sp.wait_ge(k_mm, l + 1)
                sp.wait_ge(cp_ready, l + 1)
                sp.wait_ge(rot_ready, l + 1)
                sp.wait_ge(st_ready, 4 * (l + 1))
                load_out(l)
                sp.wait_ge(ub_mm, 4 * (l + 1))
                if l == 0:
                    for n in range(DENSE):
                        if n >= NRAW:
                            raw_free(n)
                        kind, a, kh, r, w = dense_chunk(n)
                        f0 = n // HALF_CHUNKS * FF
                        if kind == "down":
                            src = ffn_d_d[0, f0 + a * P:f0 + a * P + r, :]
                            dst = raw_slot(n)[0:r, 0:w]
                        else:
                            f0 += 2 * P * a
                            src = (ffn_g_d if kind == "gate" else ffn_u_d)[0].rearrange("(k p) f -> p k f", p=P)
                            if a < MPAIRS:
                                src = src[:, 4 * kh:4 * kh + 4, f0:f0 + 2 * P]
                                dst = raw_slot(n)[:, 0:w].rearrange("p (k f) -> p k f", k=4)
                            else:
                                src = src[:, :, f0:f0 + rows(FT - 1)]
                                dst = raw_slot(n)[:, 0:w].rearrange("p (k f) -> p k f", k=KT)
                        sp.dma_start(dst, src).then_inc(raw_in[n % NRAW], 16)
                    sp.wait_ge(chunk_used, DENSE)
                    load_in(1)

            def load_expert_chunk(e, n, i):
                kind, k, r, w = exp_chunk((n - DENSE) % EXP_CHUNKS)
                src = {"gate": moe_g_d, "up": moe_u_d, "down": moe_d_d}[kind]
                if i is not None:
                    raw_free(n, i)
                sp.dma_start(raw_slot(n)[0:r, 0:w], src[e, k * P:k * P + r, :]).then_inc(raw_in[n % NRAW], 16)

            for n in range(NRAW):
                load_expert_chunk(0, DENSE + n, None)
            sp.wait_ge(ni_ready, 1)
            turns = sp.value_load(ni_sb[0:1, 0:1], min_val=NE // 2, max_val=MAXPASS * NE // 2)
            with sp.Fori(0, turns) as i:
                e0 = (i * 2) % NE
                e2 = (i * 2 + 2) % NE
                for n in range(DENSE + NRAW, DENSE + PAIR + NRAW):
                    c = n - DENSE
                    if c == 2 * KT:
                        e0 = (i * 2 + NE) % NE
                    load_expert_chunk(e0 if c < EXP_CHUNKS else e0 + 1 if c < PAIR else e2, n, i)
            last_loads = turns * (16 * PAIR // NRAW) + 16 * (DENSE // NRAW + 1)
            for k in range(KT):
                if k < NRAW:
                    sp.wait_ge(raw_in[k], last_loads)
                sp.wait_ge(h_ready, 48 + k + 1)
                sp.dma_start(y_d[:, k, :], h[:, k, :]).then_inc(out_done, 16)
            sp.wait_ge(out_done, 16 * KT)

        @block.gpsimd
        def _(pool):
            n_chain = [0]

            def link(ins):
                n_chain[0] += 1
                ins.then_inc(pool_chain, 1)
                pool.wait_ge(pool_chain, n_chain[0])

            def low(n, i=None):
                r, w = dims(n)
                hi, lo = split_slot(n)
                pool.wait_ge(hi_done, turn(n + 1, i))
                pool.tensor_tensor(lo[0:r, 0:w], raw_slot(n)[0:r, 0:w], hi[0:r, 0:w].bitcast(F32),
                                   ALU.subtract).then_inc(lo_pool, 1)

            for l in range(DEPTH):
                if l:
                    pool.wait_ge(chunk_used, DENSE)
                for r in range(2):
                    pool.dma_start(BPX[:, r, :, 0, :], b_d[l, :, r]).then_inc(prep_in, 16)
                    pool.dma_start(CPX[:, r, :, 0, :], c_d[l, :, r]).then_inc(prep_in, 16)
                pool.dma_start(glu, glu_d[l]).then_inc(mix_in, 16)
                pool.dma_start(D[:, 9216:10240], ln_d[l]).then_inc(mix_in, 16)
                pool.dma_start(wst, wst_d[l]).then_inc(mix_in, 16)
                pool.dma_start(M[0:NSAMP, 11328:11584], wss_d[l]).then_inc(mix_in, 16)
                pool.dma_start(M[0:1, 10272:11328], sbias_d[l:l + 1, :]).then_inc(mix_in, 16)
                for r in range(2):
                    pool.dma_start(S[:, r, :, 0:NCS], h0_d[l, :, r]).then_inc(mix_in, 16)
                pool.memset(M[:, 0:2048], 0.0).then_inc(set_ready, 1)
                pool.memset(S[:, :, :, NCS:NCS + 1], 0.0).then_inc(set_ready, 1)
                pool.wait_ge(a_ready, l + 1)
                er, ei = sv(12), sv(13)
                pool.memset(rot[:, 0, :, 0:1], 1.0)
                link(pool.memset(rot[:, 1, :, 0:1], 0.0))
                n = 1
                while n < NCP:
                    lo_r, lo_i = rot[:, 0, :, 0:n], rot[:, 1, :, 0:n]
                    hi_r, hi_i = rot[:, 0, :, n:2 * n], rot[:, 1, :, n:2 * n]
                    t1 = rt1[:, 0:NP * n].rearrange("p (a b) -> p a b", b=n)
                    t2 = rt2[:, 0:NP * n].rearrange("p (a b) -> p a b", b=n)
                    pool.tensor_tensor(t1, bc(ei, n), lo_i, ALU.mult)
                    pool.tensor_tensor(t2, bc(ei, n), lo_r, ALU.mult)
                    pool.tensor_tensor(hi_r, bc(er, n), lo_r, ALU.mult)
                    link(pool.tensor_tensor(hi_i, bc(er, n), lo_i, ALU.mult))
                    pool.tensor_tensor(hi_r, hi_r, t1, ALU.subtract)
                    last = pool.tensor_tensor(hi_i, hi_i, t2, ALU.add)
                    n *= 2
                    if n == NCP:
                        last.then_inc(rot_ready, 1)
                        break
                    link(last)
                    pool.tensor_tensor(sv(14), er, er, ALU.mult)
                    pool.tensor_tensor(sv(15), ei, ei, ALU.mult)
                    link(pool.tensor_tensor(sv(16), er, ei, ALU.mult))
                    pool.tensor_tensor(er, sv(14), sv(15), ALU.subtract)
                    link(pool.tensor_tensor(ei, sv(16), sv(16), ALU.add))
                pool.wait_ge(prep_in, 64 * (l + 1))
                link(pool.tensor_scalar(CPX[:, 1, :, 0, :], CPX[:, 1, :, 0, :], -1.0, None, ALU.mult))
                ar, ai = bc(sv(10), 32), bc(sv(11), 32)
                for s in range(CH):
                    re, ni = CPX[:, 0, :, s, :], CPX[:, 1, :, s, :]
                    re1, ni1 = CPX[:, 0, :, s + 1, :], CPX[:, 1, :, s + 1, :]
                    pool.tensor_tensor(ct1, ai, ni, ALU.mult)
                    pool.tensor_tensor(ct2, ai, re, ALU.mult)
                    pool.tensor_tensor(re1, ar, re, ALU.mult)
                    link(pool.tensor_tensor(ni1, ar, ni, ALU.mult))
                    pool.tensor_tensor(re1, re1, ct1, ALU.add)
                    last = pool.tensor_tensor(ni1, ni1, ct2, ALU.subtract)
                    if s < CH - 1:
                        link(last)
                    else:
                        last.then_inc(cp_ready, 1)
                pool.wait_ge(const_in, 48)
                pool.wait_ge(mix_in, 112 * (l + 1))
                up_b = upper.unsqueeze(1).to_broadcast([P, NH, QC])
                pool.tensor_tensor(wst, wst, up_b, ALU.mult).then_inc(wst_ready, 1)
                up_s = upper[0:NSAMP, 0:NSAMP].unsqueeze(1).to_broadcast([NSAMP, NH, NSAMP])
                pool.tensor_tensor(wssv, wssv, up_s, ALU.mult).then_inc(wst_ready, 1)
                pool.wait_ge(vn_ready, 3 * l + 1)
                pool.dma_start(vn_d[l], v[0:NSAMP, 0, :]).then_inc(vn_out, 16)
                pool.wait_ge(fin_ready, l + 1)
                pool.dma_start(ss_d[l], fin[:, :]).then_inc(fin_out, 16)
                pool.dma_start(sp_d[l], finp[:, :]).then_inc(fin_out, 16)
                for n in range(DENSE if l == 0 else 0):
                    if by_pool(n):
                        low(n)
            pool.wait_ge(fin_out, 32 * DEPTH)
            pool.wait_ge(vn_out, 16 * DEPTH)
            for n in range(DENSE, DENSE + AHEAD):
                if by_pool(n):
                    low(n)
            pool.wait_ge(ni_ready, 1)
            turns = pool.value_load(ni_sb[0:1, 0:1], min_val=NE // 2, max_val=MAXPASS * NE // 2)
            with pool.Fori(0, turns) as i:
                for n in range(DENSE + AHEAD, DENSE + PAIR + AHEAD):
                    if by_pool(n):
                        low(n, i)

        @block.scalar
        def _(act):
            def squares(src, dst, k0, wait):
                for k in range(src.shape[1]):
                    wait(k)
                    act.activation(dst[:, k0 + k, :], src[:, k, :], ACT.Square).then_inc(sq_ready, 1)

            def root(n, b, width, slot):
                act.wait_ge(ms_mm, n + 1)
                act.activation(rs[:, slot * T:(slot + 1) * T], bank(b), ACT.Sqrt, bias=eps[:, 0:1],
                               scale=1.0 / width).then_inc(sd_ready, 1)

            def high(n, i=None):
                r, w = dims(n)
                c = 16 * (n // NRAW + 1)
                act.wait_ge(raw_in[n % NRAW], c if i is None else i * (16 * PAIR // NRAW) + c)
                if n >= NSPLIT:
                    act.wait_ge(chunk_used, turn(n - NSPLIT + 1, i))
                act.activation(split_slot(n)[0][0:r, 0:w], raw_slot(n)[0:r, 0:w], ACT.Copy).then_inc(hi_done, 1)

            def hidden_act(hf, p):
                n = (MPAIRS + 1) * hf + p
                nb, r = (2, P) if p < MPAIRS else (1, rows(FT - 1))
                buf = (sg, rs)[n % 2][0:r, 0:nb * T].rearrange("p (b t) -> p b t", b=nb)
                act.wait_ge(chunk_used, HALF_CHUNKS * hf + min(4 * p + 4, 4 * MPAIRS + 2))
                if n >= 2:
                    act.wait_ge(hidl_ready, n - 1)
                act.activation(buf, ps[0:r, 4 * (p % 2):4 * (p % 2) + nb, 0:T], ACT.Silu).then_inc(silu_ready, 1)
                act.wait_ge(hid_ready, n + 1)
                act.activation(hid_h[0:r, 2 * p:2 * p + nb, :], buf, ACT.Copy).then_inc(hidh_ready, 1)

            act.wait_ge(dve_chain, 1)
            for l in range(DEPTH):
                if l == 0:
                    act.wait_ge(x_in, 16)
                    squares(x, h, 0, lambda k: None)
                else:
                    squares(x, h, 0, lambda k: act.wait_ge(xadd, X_DENSE[1] + k + 1))
                root(4 * l, 0, DM, 0)
                act.wait_ge(const_in, 48)
                if l:
                    act.wait_ge(chunk_used, DENSE)
                act.activation(sv(0), col(l, "log_dt", 0, 16), ACT.Exp).then_inc(dt_ready, 1)
                act.wait_ge(th_ready, l + 1)
                act.activation(sv(3), sv(1), ACT.Exp)
                act.activation(sv(4), sv(1), ACT.Exp, scale=float(CH)).then_inc(mag_ready, 1)
                act.wait_ge(ang_ready, l + 1)
                act.activation(sv(7), sv(5), ACT.Sin)
                act.activation(sv(8), sv(6), ACT.Sin).then_inc(trig_ready, 1)
                for q in range(MT):
                    act.wait_ge(ua_mm, 4 * l + q + 1)
                    act.activation(ua[:, q, :], bank(q), ACT.Copy).then_inc(ua_ready, 1)
                if l:
                    act.wait_ge(vn_out, 16)
                act.wait_ge(bp_ready, l + 1)
                act.wait_ge(ua_ready, 4 * (l + 1))
                for lag in range(CH):
                    for pp in range(4):
                        us = act.activation(ust[32 * lag:32 * lag + 32, :, pp, :],
                                            ua[32 * pp:32 * pp + 32, :, :].rearrange(
                                                "p q (c j) -> p q c j", j=CH)[:, :, :, CH - 1 - lag], ACT.Copy)
                us.then_inc(ust_ready, 1)
                for t, (_, n) in enumerate(TILES):
                    act.wait_ge(v_mm, 3 * l + t + 1)
                    act.activation(v[0:n, t, :], ps[0:n, t, :], ACT.Gelu_apprx_tanh).then_inc(v_ready, 1)
                for n in range(2 * MT):
                    r, q = divmod(n, MT)
                    act.wait_ge(bt_mm, 8 * l + n + 1)
                    act.activation(BT[:, r, 4 * q:4 * q + 4, :],
                                   ps[:, n % 4, :].rearrange("p (n s) -> p n s", n=4),
                                   ACT.Copy).then_inc(bt_ready, 1)
                for q in range(MT):
                    act.wait_ge(s_mm, 4 * l + q + 1)
                    quad = ps[:, 4:8, :] if q % 2 == 0 else ps[:, 0:4, :]
                    for r in range(2):
                        ss = act.activation(sraw[r][:, 4 * q:4 * q + 4, :], quad[:, :, r * NCH:(r + 1) * NCH], ACT.Copy)
                    ss.then_inc(s_ready, 1)
                for q in range(MT):
                    act.wait_ge(ub_mm, 4 * l + q + 1)
                    act.activation(ub[:, q, :], bank(q), ACT.Gelu_apprx_tanh).then_inc(ub_ready, 1)
                for q in range(MT):
                    act.wait_ge(y_mm, 4 * l + q + 1)
                    act.activation(ua[:, q, :], bank((q + 1) % 4), ACT.Gelu_apprx_tanh).then_inc(y_ready, 1)
                for q in range(MT):
                    act.wait_ge(glu_mm, 4 * l + q + 1)
                    if q >= 2:
                        act.wait_ge(ya_ready, 4 * l + q - 1)
                    act.activation(sg[:, (q % 2) * T:(q % 2 + 1) * T], bank(2 if q % 2 == 0 else 0),
                                   ACT.Tanh, bias=hb2[:, 4 * l + q:4 * l + q + 1],
                                   scale=0.5).then_inc(th2_ready, 1)
                squares(ub, h, MT, lambda k: act.wait_ge(yb_ready, 4 * l + k + 1))
                squares(ua, h, 0, lambda k: act.wait_ge(ya_ready, 4 * l + k + 1))
                root(4 * l + 1, 4, MIX, 1)
                root(4 * l + 2, 5, MIX, 0)
                if l == 0:
                    high(0)
                    act.wait_ge(y_mm, 4)
                    for n in range(1, 5):
                        high(n)
                squares(x, sq2, 0, lambda k: act.wait_ge(xadd, X_OUT[l] + k + 1))
                root(4 * l + 3, 6, DM, 0)
                if l == 0:
                    for k in range(KT):
                        act.wait_ge(h_ready, 16 + k + 1)
                        act.activation(h_h[:, k, :], h[:, k, :], ACT.Copy).then_inc(hh_ready, 1)
                    act.wait_ge(wo_mm, 8)
                    for n in range(5, DENSE + NSPLIT):
                        if n >= NSPLIT:
                            hf, c = divmod(n - NSPLIT, HALF_CHUNKS)
                            if c < 4 * MPAIRS and c % 4 == 3:
                                hidden_act(hf, c // 4)
                            elif c == 4 * MPAIRS + 1:
                                hidden_act(hf, MPAIRS)
                        if n < DENSE:
                            high(n)
            for n in range(3):
                high(DENSE + n)
            act.wait_ge(vn_out, 32)
            for n in range(6):
                t = n // 2
                act.wait_ge(htok_mm, n + 1)
                act.activation(tok_h[0:TILES[t][1], t, (n % 2) * 512:(n % 2 + 1) * 512],
                               ps[0:TILES[t][1], n + 1, :], ACT.Copy).then_inc(tokh_ready, 1)
            act.wait_ge(d_ready, 1)
            act.activation(e1, cn, ACT.Exp).then_inc(e_ready, 1)
            for n in range(3, AHEAD):
                high(DENSE + n)

            def gathered_act(wait):
                for b in range(2):
                    act.wait_ge(gather_mm, wait(b + 1))
                    act.activation(hg_h[:, 4 * b:4 * b + 4, :],
                                   ps[:, 6 + b, :].rearrange("p (k s) -> p k s", s=P),
                                   ACT.Copy).then_inc(hgh_ready, 1)

            def output_act():
                for b in range(2):
                    act.activation(ye_h[:, 512 * b:512 * b + 512], ps[:, 6 + b, :], ACT.Copy,
                                   scale=gslot).then_inc(yeh_ready, 1)

            gathered_act(lambda b: b)
            act.wait_ge(zero_ready, 1)
            act.wait_ge(ni_ready, 1)
            turns = act.value_load(ni_sb[0:1, 0:1], min_val=NE // 2, max_val=MAXPASS * NE // 2)
            with act.Fori(0, turns) as i:
                for a in range(2):
                    for c in range(AHEAD, EXP_CHUNKS + AHEAD):
                        n = DENSE + EXP_CHUNKS * a + c
                        if c == NSPLIT - 1:
                            act.wait_ge(chunk_used, turn(n - NSPLIT + 1, i))
                            act.wait_ge(hgl_ready, per_expert(i, a, 2, 2))
                            output_act()
                        if c == 14 + NSPLIT:
                            act.wait_ge(chunk_used, turn(n - NSPLIT + 1, i))
                            for b, (f0, f1) in enumerate(FCH):
                                act.activation(he[:, f0:f1], ps[:, b, 0:f1 - f0], ACT.Silu).then_inc(esilu_ready, 1)
                        if c == 15 + NSPLIT:
                            gathered_act(lambda b: per_expert(i, a, 2, 2 + b))
                            for b in range(3):
                                act.wait_ge(etr_mm, per_expert(i, a, 3, b + 1))
                                m = 4 if b < 2 else 2
                                hh = act.activation(het_h[:, 4 * b:4 * b + m, :],
                                                    ps[:, b, 0:m * P].rearrange("p (k s) -> p k s", s=P), ACT.Copy)
                                if b == 2:
                                    r = rows(FT - 1)
                                    hh = act.activation(het_h[0:r, FT - 1, :], ps[0:r, 2, 2 * P:3 * P], ACT.Copy)
                                hh.then_inc(heth_ready, 1)
                        high(n, i)
            act.wait_ge(chunk_used, turns * PAIR + DENSE)
            output_act()
            act.wait_ge(xadd, 16 * turns + (X_MOE + 8))
            squares(x, h, 0, lambda k: None)
            root(8, 0, DM, 0)

        @block.tensor
        def _(pe):
            def mean_sum(src, k0, n, b, need):
                for k in range(n):
                    pe.wait_ge(sq_ready, need + k + 1)
                    mm = pe.matmul(bank(b), ones, src[:, k0 + k, :], start=(k == 0), stop=(k == n - 1))
                mm.then_inc(ms_mm, 1)

            def split_mm(out, w_hi, w_lo, x_hi, x_lo, start, stop):
                pe.matmul(out, w_hi, x_hi, start=start, stop=False)
                pe.matmul(out, w_hi, x_lo, start=False, stop=False)
                return pe.matmul(out, w_lo, x_hi, start=False, stop=stop)

            pe.wait_ge(const_in, 48)
            for l in range(DEPTH):
                mean_sum(h, 0, KT, 0, 24 * l)
                for q in range(MT):
                    for k in range(KT):
                        if q == 0:
                            pe.wait_ge(h_ready, 24 * l + k + 1)
                            pe.wait_ge(w_in_in[k // 4], 16 * (l + 1))
                        mm = pe.matmul(bank(q), w_in[:, k, q * P:(q + 1) * P], h[:, k, :],
                                       start=(k == 0), stop=(k == KT - 1))
                    mm.then_inc(ua_mm, 1)
                pe.wait_ge(w_in_in[2], 16 * (l + 1))
                for t, (t0, n) in enumerate(TILES):
                    pe.wait_ge(ua_ready, 4 * l + t + 1)
                    for k in range(KT):
                        mm = pe.matmul(ps[0:n, t, :], h[:, k, t0:t0 + n], w_in[:, k, 2 * MIX:IN_W],
                                       start=(k == 0), stop=(k == KT - 1))
                    mm.then_inc(v_mm, 1)
                pe.wait_ge(bp_ready, l + 1)
                for n in range(2 * MT):
                    r, q = divmod(n, MT)
                    if n < 3:
                        pe.wait_ge(v_ready, 3 * l + n + 1)
                    elif n == 3:
                        pe.wait_ge(ua_ready, 4 * l + 4)
                    else:
                        pe.wait_ge(bt_ready, 8 * l + n - 3)
                    for pp in range(4):
                        mm = pe.transpose(bank(n % 4, P, pp * P), BPX[:, r, 4 * q + pp, :, :], ident)
                    mm.then_inc(bt_mm, 1)
                pe.wait_ge(bt_ready, 8 * (l + 1))
                pe.wait_ge(ust_ready, l + 1)
                for q in range(MT):
                    if q >= 2:
                        pe.wait_ge(s_ready, 4 * l + q - 1)
                    for pp in range(4):
                        for r in range(2):
                            mm = pe.matmul(bank(4 * ((q + 1) % 2) + pp, NCH, r * NCH),
                                           BT[:, r, 4 * q + pp, :], ust[:, q, pp, :], start=True, stop=True)
                    mm.then_inc(s_mm, 1)
                pe.wait_ge(w_in_in[3], 16 * (l + 1))
                for q in range(MT):
                    pe.wait_ge(s_ready, 4 * (l + 1))
                    for k in range(KT):
                        mm = pe.matmul(bank(q), w_in[:, k, MIX + q * P:MIX + (q + 1) * P], h[:, k, :],
                                       start=(k == 0), stop=(k == KT - 1))
                    mm.then_inc(ub_mm, 1)
                pe.wait_ge(cp_ready, l + 1)
                pe.wait_ge(ub_ready, 4 * l + 1)
                for q in range(MT):
                    for pp in range(4):
                        for r in range(2):
                            mm = pe.matmul(ps[32 * pp:32 * pp + 32, 0, q * P:(q + 1) * P],
                                           BPX[:, r, 4 * q + pp, 0, :], CPX[:, r, 4 * q + pp, 0:CH, :],
                                           start=(r == 0), stop=(r == 1))
                mm.then_inc(k_mm, 1)
                pe.wait_ge(mix_in, 112 * (l + 1))
                pe.wait_ge(wst_ready, 2 * (l + 1))
                pe.wait_ge(vn_ready, 3 * (l + 1))
                pe.wait_ge(s_ready, 4 * (l + 1))
                for ft in range(MT):
                    for hh in range(2):
                        hd = 2 * ft + hh
                        o = ps[64 * hh:64 * hh + 64, 4 + ft, :]
                        pe.matmul(o[:, 0:NSAMP].rearrange("p (b j) -> p b j", j=LS), ones[0:1, 0:HD],
                                  sbr[:, hd, 0:LS].unsqueeze(1).to_broadcast([1, BS, LS]),
                                  start=True, stop=False, skip_group_check=True)
                        pe.matmul(o[:, NSAMP:T].rearrange("p (b j) -> p b j", j=QC), ones[0:1, 0:HD],
                                  sbr[:, hd, LS:LS + QC].unsqueeze(1).to_broadcast([1, 2, QC]),
                                  start=False, stop=False, skip_group_check=True)
                        pe.matmul(o[:, 0:NSAMP], v[0:NSAMP, 0, hd * HD:(hd + 1) * HD], wssv[:, hd, :],
                                  start=False, stop=True, skip_group_check=True)
                        for t in range(1, 3):
                            t0 = TILES[t][0]
                            mm = pe.matmul(o[:, t0:t0 + P], v[:, t, hd * HD:(hd + 1) * HD], wst[:, hd, :],
                                           start=False, stop=True, skip_group_check=True)
                    mm.then_inc(sgu_mm, 1)
                pe.wait_ge(k_ready, l + 1)
                for q in range(MT):
                    pe.wait_ge(ub_ready, 4 * l + min(q + 2, 4))
                    pe.wait_ge(st_ready, 4 * l + q + 1)
                    b = (q + 1) % 4
                    uv = ua[:, q, :].rearrange("p (c j) -> p c j", j=CH)
                    yv = bank(b).rearrange("p (c j) -> p c j", j=CH)
                    for s in range(CH):
                        pe.matmul(yv[:, :, s:CH], Kt[:, q, s, :], uv[:, :, 0:CH - s],
                                  start=(s == 0), stop=False, skip_group_check=True)
                    for r in range(2):
                        for j in range(CH):
                            for pp in range(4):
                                n = 4 * q + pp
                                mm = pe.matmul(yv[32 * pp:32 * pp + 32, :, j], CPX[:, r, n, j + 1, :],
                                               S[:, r, n, 0:NCH], start=False,
                                               stop=(r == 1), skip_group_check=True)
                    mm.then_inc(y_mm, 1)
                for q in range(MT):
                    pe.wait_ge(y_ready, 4 * (l + 1))
                    if q >= 2:
                        pe.wait_ge(ya_ready, 4 * l + q - 1)
                    for z in range(2):
                        b = [1, 2][z] if q % 2 == 0 else [3, 0][z]
                        mm = pe.matmul(bank(b), glu[:, q, z, :], ua[:, q, :], start=True, stop=True)
                    mm.then_inc(glu_mm, 1)
                pe.wait_ge(yb_ready, 4 * (l + 1))
                mean_sum(h, MT, MT, 4, 24 * l + 8)
                mean_sum(h, 0, MT, 5, 24 * l + 12)
                for m in range(KT):
                    if m >= 4:
                        pe.wait_ge(xadd, X_OUT[l] + m - 3)
                    for k in range(KT):
                        if m == 0:
                            pe.wait_ge(h_ready, 24 * l + 8 + k + 1)
                            pe.wait_ge(w_out_in[k // 2], 16 * (l + 1))
                        mm = pe.matmul(bank(m % 4), w_out[:, k, m * P:(m + 1) * P], h[:, k, :],
                                       start=(k == 0), stop=(k == KT - 1))
                    mm.then_inc(wo_mm, 1)
                mean_sum(sq2, 0, KT, 6, 24 * l + 16)
                if l == 0:
                    for hf in range(2):
                        n = HALF_CHUNKS * hf
                        for p in range(MPAIRS + 1):
                            if p >= 2:
                                pe.wait_ge(hid_ready, (MPAIRS + 1) * hf + p - 1)
                            elif hf:
                                pe.wait_ge(xadd, X_DENSE[0] + 4 * (p + 1))
                            nb, r, nk = (2, P, 4) if p < MPAIRS else (1, rows(FT - 1), KT)
                            for z in range(2):
                                for k0 in range(0, KT, nk):
                                    wait_low(pe, n)
                                    w_hi, w_lo = [w[:, 0:nk * nb * r].rearrange("p (k f) -> p k f", k=nk)
                                                  for w in split_slot(n)]
                                    for m in range(nb):
                                        for k in range(nk):
                                            if n == 0 and m == 0 or n == 1 and m == 0:
                                                pe.wait_ge(hl_ready, k0 + k + 1)
                                            f = slice(m * P, m * P + r)
                                            mm = split_mm(ps[0:r, 4 * (p % 2) + 2 * z + m, 0:T],
                                                          w_hi[:, k, f], w_lo[:, k, f],
                                                          h_h[:, k0 + k, :], h_l[:, k0 + k, :],
                                                          k0 + k == 0, k0 + k == KT - 1)
                                    mm.then_inc(chunk_used, 1)
                                    n += 1
                        for kk in range(FT):
                            wait_low(pe, n)
                            pe.wait_ge(hidl_ready, (MPAIRS + 1) * hf + kk // 2 + 1)
                            w_hi, w_lo = split_slot(n)
                            r = rows(kk)
                            for m in range(KT):
                                if kk == 0 and m % 4 == 0:
                                    pe.wait_ge(hid_ready, (MPAIRS + 1) * hf + MPAIRS + m // 4)
                                f = slice(m * P, (m + 1) * P)
                                mm = split_mm(bank(m), w_hi[0:r, f], w_lo[0:r, f], hid_h[0:r, kk, :],
                                              hid_l[0:r, kk, :], kk == 0, kk == FT - 1)
                                if kk == FT - 1 and m < KT - 1:
                                    mm.then_inc(dn_mm, 1)
                            mm.then_inc(chunk_used, 1)
                            n += 1
            pe.wait_ge(h_ready, 48)
            for t, (t0, n) in enumerate(TILES):
                for k in range(KT):
                    mm = pe.matmul(ps[0:n, 0, 8 * t:8 * t + 8], h[:, k, t0:t0 + n], rw[:, k, :],
                                   start=(k == 0), stop=(k == KT - 1))
            mm.then_inc(lg_mm, 1)
            for n in range(6):
                t0, w = TILES[n // 2]
                for k in range(4):
                    mm = pe.transpose(ps[0:w, n + 1, k * P:(k + 1) * P], h[:, 4 * (n % 2) + k, t0:t0 + w], ident)
                mm.then_inc(htok_mm, 1)
            pe.wait_ge(mask_ready, 3)
            for t, (t0, n) in enumerate(TILES):
                for u in range(t + 1):
                    w = TILES[u][1]
                    lhs = strict[0:w, 0:n] if u == t else ones[0:w, 0:n]
                    pe.matmul(ps[0:n, 7, 8 * t:8 * t + 8], lhs, mask[0:w, u, :], start=(u == 0), stop=(u == t))
            for u, (_, w) in enumerate(TILES):
                mm = pe.matmul(ps[:, 7, 24:32], ones[0:w, :], mask[0:w, u, :], start=(u == 0), stop=(u == 2))
            mm.then_inc(pos_mm, 1)
            pe.wait_ge(tokl_ready, 6)

            def gather(need_oh):
                pe.wait_ge(oh_ready, need_oh)
                for k in range(KT):
                    for t in (1, 2, 0):
                        n = TILES[t][1]
                        for z, part in enumerate((tok_h, tok_l)):
                            mm = pe.matmul(bank(6 + k // 4, P, (k % 4) * P), part[0:n, t, k * P:(k + 1) * P],
                                           oh[0:n, t, :], start=(t == 1 and z == 0), stop=(t == 0 and z == 1))
                    if k % 4 == 3:
                        mm.then_inc(gather_mm, 1)

            def scatter(k, yel, add):
                if k < 2:
                    pe.wait_ge(yel_ready, yel(k + 1))
                else:
                    pe.wait_ge(xadd, add(k - 1))
                f = slice(k * P, (k + 1) * P)
                pe.matmul(bank(6 + k % 2), ye_h[:, f], sgt, start=True, stop=False)
                pe.matmul(bank(6 + k % 2), ye_l[:, f], sgt, start=False, stop=True).then_inc(sc_mm, 1)

            gather(1)
            pe.wait_ge(ni_ready, 1)
            turns = pe.value_load(ni_sb[0:1, 0:1], min_val=NE // 2, max_val=MAXPASS * NE // 2)
            with pe.Fori(0, turns) as i:
                for a in range(2):
                    n0 = DENSE + EXP_CHUNKS * a
                    for c in range(2 * KT):
                        k, z = divmod(c, 2)
                        if c == 0 or c == 8:
                            pe.wait_ge(hgl_ready, per_expert(i, a, 2, c // 8 + 1))
                        if c == 1:
                            pe.wait_ge(sgt_ready, per_expert(i, a, 1, 1))
                        wait_low(pe, n0 + c, i)
                        w_hi, w_lo = split_slot(n0 + c)
                        for b, (f0, f1) in enumerate(FCH):
                            o = ps[:, 3 * z + b, 0:f1 - f0]
                            pe.matmul(o, hg_h[:, k, :], w_hi[:, f0:f1], start=(k == 0), stop=False)
                            pe.matmul(o, hg_h[:, k, :], w_lo[:, f0:f1], start=False, stop=False)
                        for b, (f0, f1) in enumerate(FCH):
                            mm = pe.matmul(ps[:, 3 * z + b, 0:f1 - f0], hg_l[:, k, :], w_hi[:, f0:f1],
                                           start=False, stop=(k == KT - 1))
                            if c == 2 * KT - 1 and b < 2:
                                mm.then_inc(egu_mm, 1)
                        mm.then_inc(chunk_used, 1)
                        tile = k if z == 1 and k < KT - 1 else KT - 1 if c == 2 * KT - 2 else None
                        if tile is not None:
                            scatter(tile, lambda m: per_expert(i, a, 2, m),
                                    lambda m: per_expert(i, a, 8, X_MOE + m))
                    pe.wait_ge(xadd, per_expert(i, a, 8, X_MOE + 8))
                    gather(per_expert(i, a, 1, 2))
                    pe.wait_ge(he_ready, per_expert(i, a, 3, 1))
                    pe.wait_ge(goh_ready, per_expert(i, a, 1, 1))
                    for t in (1, 2, 0):
                        t0, n = TILES[t]
                        mm = pe.transpose(bank(3, n, t0), goh[0:n, t, :], ident[0:n, 0:n])
                    mm.then_inc(gtr_mm, 1)
                    for b in range(3):
                        pe.wait_ge(he_ready, per_expert(i, a, 3, b + 1))
                        for kk in range(4 * b, min(4 * b + 4, FT)):
                            r = rows(kk)
                            mm = pe.transpose(ps[0:r, b, (kk % 4) * P:(kk % 4 + 1) * P],
                                              he[:, kk * P:kk * P + r], ident)
                        mm.then_inc(etr_mm, 1)
                    pe.wait_ge(hgl_ready, per_expert(i, a, 2, 4))
                    for kk in range(FT):
                        n = n0 + 2 * KT + kk
                        if kk % 4 == 0:
                            pe.wait_ge(hetl_ready, per_expert(i, a, 3, kk // 4 + 1))
                        wait_low(pe, n, i)
                        w_hi, w_lo = split_slot(n)
                        r = rows(kk)
                        for z in range(2):
                            f = slice(512 * z, 512 * z + 512)
                            pe.matmul(ps[:, 6 + z, :], het_h[0:r, kk, :], w_hi[0:r, f], start=(kk == 0), stop=False)
                            pe.matmul(ps[:, 6 + z, :], het_h[0:r, kk, :], w_lo[0:r, f], start=False, stop=False)
                        for z in range(2):
                            f = slice(512 * z, 512 * z + 512)
                            mm = pe.matmul(ps[:, 6 + z, :], het_l[0:r, kk, :], w_hi[0:r, f], start=False,
                                           stop=(kk == FT - 1))
                        mm.then_inc(chunk_used, 1)
            for k in range(KT):
                scatter(k, lambda m: turns * 4 + m, lambda m: turns * 16 + (X_MOE + m))
            mean_sum(h, 0, KT, 0, 48)

        @block.vector
        def _(dve):
            n_chain = [0]

            def link(ins):
                n_chain[0] += 1
                ins.then_inc(dve_chain, 1)
                dve.wait_ge(dve_chain, n_chain[0])

            def tt(o, a, b, op):
                return dve.tensor_tensor(o, a, b, op)

            def normalise(n, slot, pairs):
                dve.wait_ge(sd_ready, n)
                r = rs[:, slot * T:(slot + 1) * T]
                link(dve.reciprocal(r, r))
                for dst, src, gain in pairs:
                    dve.scalar_tensor_tensor(dst, src, gain, r, ALU.mult, ALU.mult).then_inc(h_ready, 1)

            def add_to_x(k, b):
                tt(x[:, k, :], x[:, k, :], bank(b), ALU.add).then_inc(xadd, 1)

            def low(n, i=None):
                r, w = dims(n)
                hi, lo = split_slot(n)
                dve.wait_ge(hi_done, turn(n + 1, i))
                tt(lo[0:r, 0:w], raw_slot(n)[0:r, 0:w], hi[0:r, 0:w].bitcast(F32), ALU.subtract).then_inc(lo_dve, 1)

            def hidden_dve(hf, p):
                n = (MPAIRS + 1) * hf + p
                nb, r = (2, P) if p < MPAIRS else (1, rows(FT - 1))
                buf = (sg, rs)[n % 2][0:r, 0:nb * T].rearrange("p (b t) -> p b t", b=nb)
                b0 = 4 * (p % 2) + 2
                dve.wait_ge(silu_ready, n + 1)
                tt(buf, buf, ps[0:r, b0:b0 + nb, 0:T], ALU.mult).then_inc(hid_ready, 1)
                dve.wait_ge(hidh_ready, n + 1)
                tt(hid_l[0:r, 2 * p:2 * p + nb, :], buf, hid_h[0:r, 2 * p:2 * p + nb, :].bitcast(F32),
                   ALU.subtract).then_inc(hidl_ready, 1)

            link(dve.memset(eps[:, :], EPS))
            dve.wait_ge(const_in, 48)
            for l in range(DEPTH):
                dve.tensor_scalar(hb2[:, 4 * l:4 * l + 4], col(l, "glu_b2", 0, 4), 0.5, None, ALU.mult)
            for l in range(DEPTH):
                normalise(4 * l + 1, 0, [(h[:, k, :], x[:, k, :], col(l, "norm_mix", k)) for k in range(KT)])
                are, aim = col(l, "a_re", 0, 16), col(l, "a_im", 0, 16)
                dve.wait_ge(dt_ready, l + 1)
                tt(sv(1), are, sv(0), ALU.mult)
                tt(sv(2), aim, sv(0), ALU.mult).then_inc(th_ready, 1)
                dve.wait_ge(th_ready, l + 1)
                link(dve.tensor_scalar(sv(9), sv(2), 1.0 / TWO_PI, ROUND, ALU.mult, ALU.add))
                link(dve.tensor_scalar(sv(9), sv(9), ROUND, None, ALU.subtract))
                link(dve.scalar_tensor_tensor(sv(5), sv(9), -C1, sv(2), ALU.mult, ALU.add))
                link(dve.scalar_tensor_tensor(sv(5), sv(9), -C2, sv(5), ALU.mult, ALU.add))
                link(dve.tensor_scalar(sv(5), sv(5), PI_SAFE, -PI_SAFE, ALU.min, ALU.max))
                link(dve.tensor_scalar(sv(6), sv(5), -1.0, None, ALU.mult))
                link(tt(sv(6), sv(5), sv(6), ALU.min))
                dve.tensor_scalar(sv(6), sv(6), TWO_PI / 4, None, ALU.add).then_inc(ang_ready, 1)
                dve.wait_ge(mag_ready, l + 1)
                dve.wait_ge(trig_ready, l + 1)
                dve.wait_ge(ang_ready, l + 1)
                sn, cs = sv(7), sv(8)
                tt(sv(10), sv(3), cs, ALU.mult)
                tt(sv(11), sv(3), sn, ALU.mult)
                tt(sv(17), cs, cs, ALU.mult)
                tt(sv(18), sn, sn, ALU.mult)
                link(tt(sv(19), cs, sn, ALU.mult))
                tt(sv(17), sv(17), sv(18), ALU.subtract)
                link(tt(sv(19), sv(19), sv(19), ALU.add))
                tt(sv(20), sv(17), sv(17), ALU.mult)
                tt(sv(21), sv(19), sv(19), ALU.mult)
                link(tt(sv(22), sv(17), sv(19), ALU.mult))
                tt(sv(12), sv(20), sv(21), ALU.subtract)
                link(tt(sv(13), sv(22), sv(22), ALU.add))
                tt(a4[:, 0:NP], sv(4), sv(12), ALU.mult)
                tt(a4[:, NP:2 * NP], sv(4), sv(13), ALU.mult).then_inc(a_ready, 1)
                dve.wait_ge(a_ready, l + 1)
                link(dve.tensor_copy(mag_tab, bc(sv(4), NCP)))
                dve.memset(mag_tab[:, :, 0:1], 0.0)
                dve.tensor_scalar(sv(23), sv(10), -1.0, None, ALU.add)
                tt(sv(24), are, are, ALU.mult)
                link(tt(sv(25), aim, aim, ALU.mult))
                link(tt(sv(24), sv(24), sv(25), ALU.add))
                dve.reciprocal(sv(24), sv(24))
                tt(sv(26), sv(23), are, ALU.mult)
                tt(sv(27), sv(11), aim, ALU.mult)
                tt(sv(28), sv(11), are, ALU.mult)
                link(tt(sv(29), sv(23), aim, ALU.mult))
                tt(sv(26), sv(26), sv(27), ALU.add)
                link(tt(sv(28), sv(28), sv(29), ALU.subtract))
                tt(sv(26), sv(26), sv(24), ALU.mult)
                link(tt(sv(28), sv(28), sv(24), ALU.mult))
                dve.wait_ge(prep_in, 64 * (l + 1))
                for s in range(CH):
                    fr, fi = (bc(sv(26), 32), bc(sv(28), 32)) if s == 0 else (bc(sv(10), 32), bc(sv(11), 32))
                    br, bi = BPX[:, 0, :, max(s - 1, 0), :], BPX[:, 1, :, max(s - 1, 0), :]
                    o_r, o_i = BPX[:, 0, :, s, :], BPX[:, 1, :, s, :]
                    tt(bt1, fi, bi, ALU.mult)
                    link(tt(bt2, fi, br, ALU.mult))
                    tt(o_r, fr, br, ALU.mult)
                    link(tt(o_i, fr, bi, ALU.mult))
                    tt(o_r, o_r, bt1, ALU.subtract)
                    last = tt(o_i, o_i, bt2, ALU.add)
                    if s < CH - 1:
                        link(last)
                    else:
                        last.then_inc(bp_ready, 1)
                link(dve.memset(var[:, :], 1.0))
                dve.wait_ge(mix_in, 112 * (l + 1))
                for t, (_, n) in enumerate(TILES):
                    vt = v[0:n, t, :].rearrange("p (h d) -> p h d", h=NH)
                    m_, v_ = mu[0:n, 8 * t:8 * t + 8], var[0:n, 8 * t:8 * t + 8]
                    dve.wait_ge(v_ready, 3 * l + t + 1)
                    link(dve.tensor_reduce(m_, vt, AX.X, ALU.add))
                    link(dve.tensor_scalar(m_, m_, 1.0 / HD, None, ALU.mult))
                    link(tt(vt, vt, bc(m_, HD), ALU.subtract))
                    sqv = lt[0:n, :].rearrange("p (h d) -> p h d", h=NH)
                    link(tt(sqv, vt, vt, ALU.mult))
                    link(dve.tensor_reduce(v_, sqv, AX.X, ALU.add))
                link(dve.tensor_scalar(var[:, :], var[:, :], 1.0 / HD, EPS, ALU.mult, ALU.add))
                yi, yt = nwt[:, 0:24], nwt[:, 24:48]
                link(dve.tensor_scalar(yi.bitcast(I32), var[:, :].bitcast(I32), 1, None, ALU.logical_shift_right))
                link(dve.tensor_scalar(yi.bitcast(I32), yi.bitcast(I32), -1.0, float(0x5F3759DF), ALU.mult, ALU.add))
                for _ in range(4):
                    link(tt(yt, yi, yi, ALU.mult))
                    link(tt(yt, yt, var[:, :], ALU.mult))
                    link(dve.tensor_scalar(yt, yt, -0.5, 1.5, ALU.mult, ALU.add))
                    link(tt(yi, yi, yt, ALU.mult))
                for t, (_, n) in enumerate(TILES):
                    vt = v[0:n, t, :].rearrange("p (h d) -> p h d", h=NH)
                    link(tt(vt, vt, bc(nwt[0:n, 8 * t:8 * t + 8], HD), ALU.mult))
                    link(tt(v[0:n, t, :], v[0:n, t, :], lng[0:n, :], ALU.mult))
                    tt(v[0:n, t, :], v[0:n, t, :], lnb[0:n, :], ALU.add).then_inc(vn_ready, 1)
                dve.wait_ge(rot_ready, l + 1)
                dve.wait_ge(set_ready, 2 * (l + 1))
                if l:
                    dve.wait_ge(fin_out, 32 * l)
                f_r = fin[:, 0:128].rearrange("p (n c) -> p n c", n=NP)
                f_i = fin[:, 128:256].rearrange("p (n c) -> p n c", n=NP)
                h0r, h0i = S[:, 0, :, 0:NCS], S[:, 1, :, 0:NCS]
                a4r, a4i = bc(a4[:, 0:NP], NCS), bc(a4[:, NP:2 * NP], NCS)
                t8a = lt[:, 0:128].rearrange("p (n c) -> p n c", n=NP)
                t8b = lt[:, 128:256].rearrange("p (n c) -> p n c", n=NP)
                tt(f_r, a4r, h0r, ALU.mult)
                tt(f_i, a4r, h0i, ALU.mult)
                tt(t8a, a4i, h0i, ALU.mult)
                link(tt(t8b, a4i, h0r, ALU.mult))
                tt(f_r, f_r, t8a, ALU.subtract)
                link(tt(f_i, f_i, t8b, ALU.add))

                def v4(ap):
                    return ap.rearrange("p (n c) -> p n c", n=4)

                for q in range(MT):
                    if q:
                        dve.wait_ge(st_ready, 4 * l + q)
                    dve.wait_ge(s_ready, 4 * l + q + 1)
                    n4 = slice(4 * q, 4 * q + 4)
                    sr, si = sraw[0][:, n4, NCS:NCH], sraw[1][:, n4, NCS:NCH]
                    cr, ci = rot[:, 0, n4, :], rot[:, 1, n4, :]
                    tt(f_r[:, n4, :], f_r[:, n4, :], sraw[0][:, n4, 0:NCS], ALU.add)
                    tt(f_i[:, n4, :], f_i[:, n4, :], sraw[1][:, n4, 0:NCS], ALU.add)
                    tt(v4(wr), sr, cr, ALU.mult)
                    link(tt(v4(tmp), si, ci, ALU.mult))
                    link(tt(wr, wr, tmp, ALU.add))
                    tt(v4(wi), si, cr, ALU.mult)
                    link(tt(v4(tmp), sr, ci, ALU.mult))
                    link(tt(wi, wi, tmp, ALU.subtract))
                    mg = mag_tab[:, n4, :].rearrange("p n c -> p (n c)")
                    dve.tensor_tensor_scan(wr, mg, wr, 0.0, ALU.mult, ALU.add)
                    link(dve.tensor_tensor_scan(wi, mg, wi, 0.0, ALU.mult, ALU.add))
                    or_, oi = S[:, 0, n4, NCS + 1:NCH + 1], S[:, 1, n4, NCS + 1:NCH + 1]
                    tt(or_, v4(wr), cr, ALU.mult)
                    link(tt(v4(tmp), v4(wi), ci, ALU.mult))
                    link(tt(or_, or_, v4(tmp), ALU.subtract))
                    tt(oi, v4(wi), cr, ALU.mult)
                    link(tt(v4(tmp), v4(wr), ci, ALU.mult))
                    tt(oi, oi, v4(tmp), ALU.add).then_inc(st_ready, 1)
                    if q == 1:
                        dve.wait_ge(k_mm, l + 1)
                        for pp in range(4):
                            a, b = 32 * pp, 32 * pp + 32
                            last = dve.tensor_copy(Kt[a:b, :, :, a:b],
                                                   ps[a:b, 0, :].rearrange("p (q s f) -> p q s f", q=MT, s=CH))
                        link(last)
                        for k in range(MT):
                            last = dve.scalar_tensor_tensor(Kt[:, k, 0, :], ident, col(l, "ssm_d", k), Kt[:, k, 0, :],
                                                            ALU.mult, ALU.add)
                        last.then_inc(k_ready, 1)
                dve.wait_ge(st_ready, 4 * (l + 1))
                dve.tensor_copy(finp[:, 0:NP], S[:, 0, :, NCH])
                dve.tensor_copy(finp[:, NP:2 * NP], S[:, 1, :, NCH]).then_inc(fin_ready, 1)
                for ft in range(MT):
                    dve.wait_ge(sgu_mm, 4 * l + ft + 1)
                    dve.wait_ge(ub_ready, 4 * l + ft + 1)
                    tt(ub[:, ft, :], ub[:, ft, :], bank(4 + ft), ALU.mult).then_inc(yb_ready, 1)
                for q in range(MT):
                    dve.wait_ge(th2_ready, 4 * l + q + 1)
                    s_ = sg[:, (q % 2) * T:(q % 2 + 1) * T]
                    link(dve.tensor_scalar(s_, s_, 0.5, 0.5, ALU.mult, ALU.add))
                    dve.scalar_tensor_tensor(ua[:, q, :], bank(1 if q % 2 == 0 else 3), col(l, "glu_b1", q), s_,
                                             ALU.add, ALU.mult).then_inc(ya_ready, 1)
                dve.wait_ge(ya_ready, 4 * (l + 1))
                dve.wait_ge(yb_ready, 4 * (l + 1))
                for slot, n in ((1, 2), (0, 3)):
                    dve.wait_ge(sd_ready, 4 * l + n)
                    last = dve.reciprocal(rs[:, slot * T:(slot + 1) * T], rs[:, slot * T:(slot + 1) * T])
                link(last)
                for k in range(KT):
                    src, gain = (ua, "out_norm_a") if k < MT else (ub, "out_norm_b")
                    slot = 0 if k < MT else 1
                    dve.scalar_tensor_tensor(h[:, k, :], src[:, k % MT, :], col(l, gain, k % MT),
                                             rs[:, slot * T:(slot + 1) * T],
                                             ALU.mult, ALU.mult).then_inc(h_ready, 1)
                for n in range(0 if l else 5):
                    if not by_pool(n):
                        low(n)
                for m in range(KT):
                    dve.wait_ge(wo_mm, 8 * l + m + 1)
                    add_to_x(m, m % 4)
                dve.wait_ge(xadd, X_OUT[l] + 8)
                normalise(4 * l + 4, 0, [(h[:, k, :], x[:, k, :], col(l, "norm_ffn", k)) for k in range(KT)])
                if l == 0:
                    for k in range(KT):
                        dve.wait_ge(hh_ready, k + 1)
                        tt(h_l[:, k, :], h[:, k, :], h_h[:, k, :].bitcast(F32), ALU.subtract).then_inc(hl_ready, 1)
                    for n in range(5, DENSE + NSPLIT):
                        if n >= NSPLIT:
                            hf, c = divmod(n - NSPLIT, HALF_CHUNKS)
                            if c < 4 * MPAIRS and c % 4 == 3:
                                hidden_dve(hf, c // 4)
                            elif c == 4 * MPAIRS + 1:
                                hidden_dve(hf, MPAIRS)
                            elif c == HALF_CHUNKS - 1:
                                for m in range(KT):
                                    if m < KT - 1:
                                        dve.wait_ge(dn_mm, (KT - 1) * hf + m + 1)
                                    else:
                                        dve.wait_ge(chunk_used, HALF_CHUNKS * (hf + 1))
                                    dve.wait_ge(xadd, X_DENSE[0] + 8 * hf)
                                    add_to_x(m, m)
                        if n < DENSE and not by_pool(n):
                            low(n)
                    dve.wait_ge(xadd, X_DENSE[1] + 8)
            for ap in (small[:, :], postab[:, :], gatetab[:, :]):
                last = dve.memset(ap, 0.0)
            link(last)
            for n in range(3):
                low(DENSE + n)
            dve.wait_ge(lg_mm, 1)
            for t, (_, n) in enumerate(TILES):
                last = tt(lg[0:n, t, :], ps[0:n, 0, 8 * t:8 * t + 8], rb[0:n, :], ALU.add)
            link(last)
            for t, (_, n) in enumerate(TILES):
                last = dve.max(m8[0:n, t, :], lg[0:n, t, :])
            link(last)
            for t, (_, n) in enumerate(TILES):
                dve.max_index(ixv[0:n, t, :], m8[0:n, t, :], lg[0:n, t, :])
            tt(cn, m8[:, :, 1], m8[:, :, 0], ALU.subtract).then_inc(d_ready, 1)
            dve.wait_ge(e_ready, 1)
            dve.wait_ge(d_ready, 1)
            link(dve.tensor_scalar(w0, e1, 1.0, None, ALU.add))
            link(dve.reciprocal(w0, w0))
            link(tt(w1, w0, e1, ALU.mult))
            i8 = iota[:, 0:NE]
            for t, (_, n) in enumerate(TILES):
                last = dve.tensor_copy(ixf[0:n, t, 0:2], ixv[0:n, t, 0:2])
            link(last)
            for t, (_, n) in enumerate(TILES):
                i0, i1 = ixf[0:n, t, 0:1], ixf[0:n, t, 1:2]
                dve.tensor_scalar(mask[0:n, t, :], i8[0:n, :], i0, None, ALU.is_equal)
                last = dve.tensor_scalar(r8[0:n, t, :], i8[0:n, :], i1, None, ALU.is_equal)
            link(last)
            for t, (_, n) in enumerate(TILES):
                tt(mask[0:n, t, :], mask[0:n, t, :], r8[0:n, t, :], ALU.add).then_inc(mask_ready, 1)
            for t, (_, n) in enumerate(TILES):
                last = dve.tensor_scalar(gts[0:n, t, :], i8[0:n, :], ixf[0:n, t, 0:1], w0[0:n, t:t + 1],
                                         ALU.is_equal, ALU.mult)
            link(last)
            for t, (_, n) in enumerate(TILES):
                last = dve.scalar_tensor_tensor(gts[0:n, t, :], r8[0:n, t, :], w1[0:n, t:t + 1], gts[0:n, t, :],
                                                ALU.mult, ALU.add)
            link(last)
            for n in range(6):
                t, f = n // 2, slice((n % 2) * 512, (n % 2 + 1) * 512)
                w = TILES[t][1]
                dve.wait_ge(tokh_ready, n + 1)
                tt(tok_l[0:w, t, f], ps[0:w, n + 1, :], tok_h[0:w, t, f].bitcast(F32),
                   ALU.subtract).then_inc(tokl_ready, 1)
            dve.wait_ge(mask_ready, 3)
            dve.wait_ge(pos_mm, 1)
            link(dve.tensor_reduce(cn[:, 0:1], ps[:, 7, 24:32], AX.X, ALU.max))
            dve.tensor_scalar(cn[:, 1:2], cn[:, 0:1], 128.0, 4.0, ALU.is_gt, ALU.mult)
            link(dve.tensor_scalar(cn[:, 2:3], cn[:, 0:1], 256.0, 4.0, ALU.is_gt, ALU.mult))
            link(tt(cn[:, 1:2], cn[:, 1:2], cn[:, 2:3], ALU.add))
            dve.tensor_scalar(ni_sb[:, :], cn[:, 1:2], 4.0, None, ALU.add).then_inc(ni_ready, 1)
            for t, (_, n) in enumerate(TILES):
                link(dve.tensor_scalar(r8[0:n, t, :], mask[0:n, t, :], 1000.0, -1000.0, ALU.mult, ALU.add))
                link(tt(r8[0:n, t, :], r8[0:n, t, :], ps[0:n, 7, 8 * t:8 * t + 8], ALU.add))
                for r in range(MAXPASS):
                    dve.tensor_scalar(pos[0:n, t, NE * r:NE * r + NE], r8[0:n, t, :], -128.0 * r, None, ALU.add)
                    last = dve.tensor_copy(gat[0:n, t, NE * r:NE * r + NE], gts[0:n, t, :])
            link(last)

            dve.memset(gslot, 0.0).then_inc(zero_ready, 1)
            dve.memset(sgt.bitcast(F32), 0.0).then_inc(sgt_ready, 1)

            def one_hots(i):
                for t, (_, n) in enumerate(TILES):
                    last = dve.tensor_scalar(oh[0:n, t, :], iota[0:n, :], pos[0:n, t, bass.ds(i, 1)], None,
                                             ALU.is_equal)
                last.then_inc(oh_ready, 1)

            def gated_one_hots(i):
                for t, (_, n) in enumerate(TILES):
                    last = dve.tensor_scalar(goh[0:n, t, :], iota[0:n, :], pos[0:n, t, bass.ds(i, 1)],
                                             gat[0:n, t, bass.ds(i, 1)], ALU.is_equal, ALU.mult)
                last.then_inc(goh_ready, 1)

            def gathered_dve(wait):
                for b in range(2):
                    dve.wait_ge(hgh_ready, wait(b + 1))
                    o = slice(4 * b, 4 * b + 4)
                    tt(hg_l[:, o, :], ps[:, 6 + b, :].rearrange("p (k s) -> p k s", s=P),
                       hg_h[:, o, :].bitcast(F32), ALU.subtract).then_inc(hgl_ready, 1)

            def output_dve(wait):
                for b in range(2):
                    f = slice(512 * b, 512 * b + 512)
                    dve.wait_ge(yeh_ready, wait(b + 1))
                    dve.scalar_tensor_tensor(ye_l[:, f], ps[:, 6 + b, :], gslot, ye_h[:, f].bitcast(F32),
                                             ALU.mult, ALU.subtract).then_inc(yel_ready, 1)

            def add_scattered(k, sc, before):
                dve.wait_ge(sc_mm, sc)
                dve.wait_ge(xadd, before)
                add_to_x(k, 6 + k % 2)

            one_hots(0)
            for n in range(3, AHEAD):
                if not by_pool(DENSE + n):
                    low(DENSE + n)
            gathered_dve(lambda b: b)
            dve.wait_ge(ni_ready, 1)
            dve.wait_ge(zero_ready, 1)
            turns = dve.value_load(ni_sb[0:1, 0:1], min_val=NE // 2, max_val=MAXPASS * NE // 2)
            scatter_at = {2 * k + 1 + NSPLIT: k for k in range(KT - 1)}
            scatter_at[2 * KT - 2 + NSPLIT] = KT - 1
            with dve.Fori(0, turns) as i:
                for a in range(2):
                    for c in range(AHEAD, EXP_CHUNKS + AHEAD):
                        n = DENSE + EXP_CHUNKS * a + c
                        if c == NSPLIT - 1:
                            output_dve(lambda b: per_expert(i, a, 2, b))
                        if c in scatter_at:
                            k = scatter_at[c]
                            add_scattered(k, per_expert(i, a, 8, k + 1), per_expert(i, a, 8, X_MOE - 8 + k + 1))
                        if c == 12:
                            one_hots(i * 2 + (a + 1))
                        if c == 14:
                            gated_one_hots(i * 2 + a)
                        if c == 15 + NSPLIT:
                            for b, (f0, f1) in enumerate(FCH):
                                dve.wait_ge(esilu_ready, per_expert(i, a, 3, b + 1))
                                if b < 2:
                                    dve.wait_ge(egu_mm, per_expert(i, a, 2, b + 1))
                                else:
                                    dve.wait_ge(chunk_used, turn(n - NSPLIT + 1, i))
                                tt(he[:, f0:f1], he[:, f0:f1], ps[:, 3 + b, 0:f1 - f0], ALU.mult).then_inc(he_ready, 1)
                            gathered_dve(lambda b: per_expert(i, a, 2, 2 + b))
                            for b in range(3):
                                dve.wait_ge(heth_ready, per_expert(i, a, 3, b + 1))
                                m = 4 if b < 2 else 2
                                o = slice(4 * b, 4 * b + m)
                                lo_ = tt(het_l[:, o, :], ps[:, b, 0:m * P].rearrange("p (k s) -> p k s", s=P),
                                         het_h[:, o, :].bitcast(F32), ALU.subtract)
                                if b == 2:
                                    r = rows(FT - 1)
                                    lo_ = tt(het_l[0:r, FT - 1, :], ps[0:r, 2, 2 * P:3 * P],
                                             het_h[0:r, FT - 1, :].bitcast(F32), ALU.subtract)
                                lo_.then_inc(hetl_ready, 1)
                            dve.wait_ge(gtr_mm, per_expert(i, a, 1, 1))
                            dve.tensor_reduce(gslot, bank(3), AX.X, ALU.add)
                            dve.tensor_scalar(sgt, bank(3), 0.0, None, ALU.is_gt).then_inc(sgt_ready, 1)
                        if not by_pool(n):
                            low(n, i)
            output_dve(lambda b: turns * 4 + b)
            for k in range(KT):
                add_scattered(k, turns * 16 + (k + 1), turns * 16 + (X_MOE - 8 + k + 1))
            dve.wait_ge(xadd, turns * 16 + (X_MOE + 8))
            normalise(9, 0, [(h[:, k, :], x[:, k, :], cols[:, DEPTH * NCOL + k:DEPTH * NCOL + k + 1])
                             for k in range(KT)])



def _by_feature(a, n):
    return a.reshape(n, P).T


def _pair_blocks(a):
    out = np.zeros((P, NP, 2 * GH), np.float32)
    for g in range(2):
        out[g * NST:(g + 1) * NST, :, g * GH:(g + 1) * GH] = a[g::2].transpose(1, 0, 2)
    return out


def _by_state(a):
    return np.moveaxis(a.reshape((NP, 2 * NST) + a.shape[2:]), 0, 1)


def kernel(**inputs):
    import concourse.bacc as bacc
    from concourse.bass_utils import run_bass_kernel_spmd as run

    w = {k: np.asarray(a) for k, a in inputs.items()}
    f = np.float32
    tokens = np.concatenate([w["x_sample"].reshape(NSAMP, DM), w["x_prompt"].reshape(NPROMPT, DM)])
    d = {}
    d["x"] = tokens.T.reshape(KT, P, T).transpose(1, 0, 2)
    r = np.arange(P)
    d["consts"] = np.concatenate([np.eye(P, dtype=f), (r[:, None] <= r[None, :]).astype(f),
                                  (r[:, None] < r[None, :]).astype(f),
                                  np.broadcast_to(r[None, :].astype(f), (P, P)), np.ones((P, P), f)], 1)
    cols = []
    glu = np.zeros((DEPTH, P, MT, 2, P), f)
    for l in range(DEPTH):
        b = w["glu_b"][l]
        cols += [_by_feature(w["norm_mix"][l], KT), _by_feature(w["out_norm_a"][l], MT),
                 _by_feature(w["out_norm_b"][l], MT), _by_feature(w["norm_ffn"][l], KT),
                 _by_feature(b[:, :GH].reshape(-1), MT), _by_feature(b[:, GH:].reshape(-1), MT),
                 _by_feature(w["ssm_d"][l].reshape(-1), MT),
                 _by_state(w["ssm_a_re"][l]), _by_state(w["ssm_a_im"][l]),
                 _by_state(np.repeat(w["ssm_log_dt"][l][:, None], NST, 1))]
        gw = w["glu_w"][l].reshape(MT, 8, GH, 2, GH)
        for g in range(8):
            glu[l, g * GH:(g + 1) * GH, :, :, g * GH:(g + 1) * GH] = gw[:, g].transpose(1, 0, 2, 3)
    cols.append(_by_feature(w["norm_final"], KT))
    d["cols"] = np.concatenate(cols, 1)
    d["misc"] = np.concatenate([w["router_w"][0].reshape(KT, P, NE).transpose(1, 0, 2).reshape(P, KT * NE),
                                np.broadcast_to(w["router_b"][0][None, :], (P, NE))], 1)
    d["w_in"], d["w_out"] = w["w_in"], w["w_out"]
    d["b"] = np.stack([np.stack([_pair_blocks(w["ssm_b_re"][l]), _pair_blocks(w["ssm_b_im"][l])], 1)
                       for l in range(DEPTH)])
    d["c"] = np.stack([np.stack([_pair_blocks(w["ssm_c_re"][l].transpose(0, 2, 1)),
                                 _pair_blocks(w["ssm_c_im"][l].transpose(0, 2, 1))], 1)
                       for l in range(DEPTH)])
    d["glu"] = glu
    d["ln"] = np.broadcast_to(np.concatenate([w["sgu_ln_g"].reshape(DEPTH, MIX), w["sgu_ln_b"].reshape(DEPTH, MIX)],
                                             1)[:, None, :], (DEPTH, P, 2 * MIX))
    wt = w["sgu_w"].transpose(0, 3, 1, 2)
    d["wst"] = wt
    wss = np.zeros((DEPTH, BS, LS, NH, BS, LS), f)
    for b in range(BS):
        wss[:, b, :, :, b, :] = wt[:, :LS, :, :LS]
    d["wss"] = wss.reshape(DEPTH, NSAMP, NH * NSAMP)
    d["sbias"] = np.concatenate([w["sgu_b"][:, :, :LS], w["sgu_b"]], 2).reshape(DEPTH, NH * (LS + QC))
    h0 = []
    for l in range(DEPTH):
        h0.append(np.stack([_by_state(w[n][l].transpose(1, 2, 0)) for n in ("state_ssm_re", "state_ssm_im")], 1))
    d["h0"] = np.stack(h0)
    for n in ("ffn_w_gate", "ffn_w_up", "ffn_w_down"):
        d[n] = w[n]
    for n in ("moe_w_gate", "moe_w_up", "moe_w_down"):
        d[n] = w[n][0]

    nc = bacc.Bacc("TRN2", target_bir_lowering=False, num_devices=1)
    arrays, args = {}, []
    for name, a in d.items():
        a = np.ascontiguousarray(a)
        arrays[f"in_{name}"] = a
        args.append(nc.dram_tensor(f"in_{name}", list(a.shape), F32, kind="ExternalInput").ap())
    outs = {"y": (P, KT, T), "sp": (DEPTH, P, 2 * NP), "ss": (DEPTH, P, 2 * NP * NCS), "vn": (DEPTH, NSAMP, MIX)}
    for name, shape in outs.items():
        args.append(nc.dram_tensor(f"out_{name}", list(shape), F32, kind="ExternalOutput").ap())
    build(nc, *args)
    res = run(nc, [arrays], core_ids=[0]).results[0]

    y = np.asarray(res["out_y"]).transpose(2, 1, 0).reshape(T, DM)
    sp = np.asarray(res["out_sp"]).reshape(DEPTH, 2, NST, 2, NP)
    ss = np.asarray(res["out_ss"]).reshape(DEPTH, 2, NST, 2, NP, BS)
    sp = sp.transpose(3, 0, 4, 1, 2).reshape(2, DEPTH, 1, NG, NST)
    ss = ss.transpose(3, 0, 5, 4, 1, 2).reshape(2, DEPTH, BS, NG, NST)
    vn = np.asarray(res["out_vn"]).reshape(DEPTH, BS, LS, NH, HD)
    return (np.ascontiguousarray(y[NSAMP:]).reshape(1, NPROMPT, DM), np.ascontiguousarray(y[:NSAMP]).reshape(BS, LS, DM),
            np.ascontiguousarray(sp[0]), np.ascontiguousarray(sp[1]),
            np.ascontiguousarray(ss[0]), np.ascontiguousarray(ss[1]), np.ascontiguousarray(vn))
```
